# Optimizing a Trainium2 kernel written in Bass

```python
import jax, jax.numpy as jnp
from jax import lax
import numpy as np

D_MODEL = 1024
BATCH = 1
SEQ = 1024
DEPTH = 1
DEC_BATCH = 1
DEC_SEQ = 64
PAST_LEN = 1024

CHUNK = 64
WINDOW = 128
WINDOW_CHUNKS = WINDOW // CHUNK
HEAD_DIM = 64
ATTN_HEADS = 8
KV_HEADS = 2
ATTN_GROUP = ATTN_HEADS // KV_HEADS
RET_HEADS = 8
RET_HEAD_DIM = 64
ATTN_WIDTH = ATTN_HEADS * HEAD_DIM
KV_WIDTH = KV_HEADS * HEAD_DIM
RET_WIDTH = RET_HEADS * RET_HEAD_DIM
MIX_WIDTH = ATTN_WIDTH + RET_WIDTH
IN_WIDTH = ATTN_WIDTH + 2 * KV_WIDTH + 4 * RET_WIDTH
PEER_HEADS = 8
PEER_KEYS = 128
PEER_EXPERTS = PEER_KEYS * PEER_KEYS
PEER_QDIM = 256
PEER_HALF = PEER_QDIM // 2
PEER_TOPK = 16
PEER_BLOCK = 128
EPS = 1e-6
NEG_INF = -1e30

kernel_name = "hymba_swa_retention_peer_stream_step"

def rms_norm(x, g):
    xf = x.astype(jnp.float32)
    y = xf * lax.rsqrt(jnp.mean(xf * xf, axis=-1, keepdims=True) + EPS)
    return (y * g.astype(jnp.float32)).astype(x.dtype)

def alibi_slopes():
    return jnp.asarray(2.0 ** (-8.0 * np.arange(1, ATTN_HEADS + 1) / ATTN_HEADS), dtype=jnp.float32)

def retention_log_decay():
    return jnp.asarray(np.log(1.0 - 2.0 ** (-5.0 - np.arange(RET_HEADS))), dtype=jnp.float32)

def window_attention(q, k_buf, v_buf, pos0, sinks):
    B, T = q.shape[0], q.shape[1]
    L = min(T, CHUNK)
    NB = T // L
    LK = WINDOW + L
    qb = q.reshape(B, NB, L, KV_HEADS, ATTN_GROUP, HEAD_DIM)
    idx = jnp.arange(NB)[:, None] * L + jnp.arange(LK)[None, :]
    kb = k_buf[:, idx]
    vb = v_buf[:, idx]
    q_pos = pos0 + jnp.arange(T).reshape(NB, L)
    k_pos = pos0 - WINDOW + idx
    q_chunk = q_pos // CHUNK
    k_chunk = k_pos // CHUNK
    valid = ((k_pos[:, None, :] >= 0)
             & (k_chunk[:, None, :] <= q_chunk[:, :, None])
             & (k_chunk[:, None, :] >= q_chunk[:, :, None] - WINDOW_CHUNKS))
    dist = jnp.abs(q_pos[:, :, None] - k_pos[:, None, :]).astype(jnp.float32)
    slopes = alibi_slopes().reshape(KV_HEADS, ATTN_GROUP)
    s = jnp.einsum('bnqkgd,bnskd->bnkgqs', qb, kb).astype(jnp.float32) * (HEAD_DIM ** -0.5)
    s = s - slopes[None, None, :, :, None, None] * dist[None, :, None, None, :, :]
    s = jnp.where(valid[None, :, None, None, :, :], s, NEG_INF)
    sink = jnp.broadcast_to(
        sinks.astype(jnp.float32).reshape(KV_HEADS, ATTN_GROUP)[None, None, :, :, None, None],
        s.shape[:-1] + (1,))
    p = jax.nn.softmax(jnp.concatenate([s, sink], axis=-1), axis=-1)[..., :-1]
    o = jnp.einsum('bnkgqs,bnskd->bnqkgd', p.astype(vb.dtype), vb)
    return o.reshape(B, T, ATTN_WIDTH)

def retention(q, k, v, s0):
    f32 = jnp.float32
    B, T = q.shape[0], q.shape[1]
    L = min(T, CHUNK)
    NB = T // L
    qb = q.astype(f32).reshape(B, NB, L, RET_HEADS, RET_HEAD_DIM)
    kb = k.astype(f32).reshape(B, NB, L, RET_HEADS, RET_HEAD_DIM) * (RET_HEAD_DIM ** -0.5)
    vb = v.astype(f32).reshape(B, NB, L, RET_HEADS, RET_HEAD_DIM)
    lg = retention_log_decay()
    i = jnp.arange(L, dtype=f32)
    decay_intra = jnp.exp(jnp.abs(i[:, None] - i[None, :])[None] * lg[:, None, None])
    decay_in = jnp.exp((i + 1.0)[None, :] * lg[:, None])
    decay_out = jnp.exp((L - 1.0 - i)[None, :] * lg[:, None])
    decay_block = jnp.exp(L * lg)[None, :, None, None]
    scores = jnp.einsum('bnihd,bnjhd->bnhij', qb, kb) * decay_intra
    intra = jnp.einsum('bnhij,bnjhe->bnihe', scores, vb)
    kv = jnp.einsum('bnjhd,hj,bnjhe->nbhde', kb, decay_out, vb)

    def step(S, kv_n):
        return decay_block * S + kv_n, S

    s_final, s_prev = lax.scan(step, s0.astype(f32), kv)
    cross = jnp.einsum('bnihd,hi,nbhde->bnihe', qb, decay_in, s_prev)
    return (intra + cross).reshape(B, T, RET_HEADS, RET_HEAD_DIM), s_final

def head_norm(o, g):
    mu = jnp.mean(o, axis=-1, keepdims=True)
    var = jnp.mean(jnp.square(o - mu), axis=-1, keepdims=True)
    y = (o - mu) * lax.rsqrt(var + EPS)
    return y.reshape(o.shape[0], o.shape[1], RET_WIDTH) * g.astype(jnp.float32)

def peer(x, w_q, sub_keys, u_table, v_table):
    shape = x.shape
    xt = x.reshape(-1, D_MODEL)
    n_tok = xt.shape[0]
    pad = (-n_tok) % PEER_BLOCK
    xb = jnp.pad(xt, ((0, pad), (0, 0))).reshape(-1, PEER_BLOCK, D_MODEL)

    def block(xblk):
        q = (xblk @ w_q).reshape(PEER_BLOCK, PEER_HEADS, 2, PEER_HALF)
        s = jnp.einsum('thcd,hcnd->thcn', q, sub_keys).astype(jnp.float32)
        sv, si = lax.top_k(s, PEER_TOPK)
        cand = sv[:, :, 0, :, None] + sv[:, :, 1, None, :]
        cidx = si[:, :, 0, :, None] * PEER_KEYS + si[:, :, 1, None, :]
        cand = cand.reshape(PEER_BLOCK, PEER_HEADS, PEER_TOPK * PEER_TOPK)
        cidx = cidx.reshape(PEER_BLOCK, PEER_HEADS, PEER_TOPK * PEER_TOPK)
        top_s, pos = lax.top_k(cand, PEER_TOPK)
        expert = jnp.take_along_axis(cidx, pos, axis=-1)
        g = jax.nn.softmax(top_s, axis=-1)
        u = u_table[expert]
        hid = jax.nn.gelu(jnp.einsum('thkd,td->thk', u, xblk).astype(jnp.float32), approximate=False)
        v = v_table[expert]
        return jnp.einsum('thk,thkd->td', (g * hid).astype(xblk.dtype), v)

    out = lax.map(block, xb).reshape(-1, D_MODEL)[:n_tok]
    return out.reshape(shape)

def trunk_layer(x, k_cache, v_cache, s0, pos0, attn_norm_g, w_in, attn_sinks, ret_norm_g, w_out,
                ffn_norm_g, peer_w_q, peer_sub_keys, peer_u, peer_v):
    B, T = x.shape[0], x.shape[1]
    h = rms_norm(x, attn_norm_g)
    proj = h @ w_in
    splits = np.cumsum([ATTN_WIDTH, KV_WIDTH, KV_WIDTH, RET_WIDTH, RET_WIDTH, RET_WIDTH]).tolist()
    q_a, k_a, v_a, q_r, k_r, v_r, gate = jnp.split(proj, splits, axis=-1)
    k_buf = jnp.concatenate([k_cache.astype(x.dtype), k_a.reshape(B, T, KV_HEADS, HEAD_DIM)], axis=1)
    v_buf = jnp.concatenate([v_cache.astype(x.dtype), v_a.reshape(B, T, KV_HEADS, HEAD_DIM)], axis=1)
    o_a = window_attention(q_a, k_buf, v_buf, pos0, attn_sinks)
    o_r, s_new = retention(q_r.reshape(B, T, RET_HEADS, RET_HEAD_DIM),
                           k_r.reshape(B, T, RET_HEADS, RET_HEAD_DIM),
                           v_r.reshape(B, T, RET_HEADS, RET_HEAD_DIM), s0)
    o_r = head_norm(o_r, ret_norm_g) * jax.nn.silu(gate.astype(jnp.float32))
    mixed = jnp.concatenate([o_a, o_r.astype(x.dtype)], axis=-1)
    x = x + mixed @ w_out
    x = x + peer(rms_norm(x, ffn_norm_g), peer_w_q, peer_sub_keys, peer_u, peer_v)
    return x, k_buf[:, -WINDOW:], v_buf[:, -WINDOW:], s_new.astype(s0.dtype)

def setup_inputs(seed: int = 0) -> dict:
    key = jax.random.key(seed)
    ks = jax.random.split(key, 18)
    f32 = jnp.float32
    nrm = lambda k, shape, scale: jax.random.normal(k, shape, f32) * scale
    return {
        "x_prompt": nrm(ks[0], (BATCH, SEQ, D_MODEL), 1.0),
        "x_sample": nrm(ks[1], (DEC_BATCH, DEC_SEQ, D_MODEL), 1.0),
        "cache_attn_k": nrm(ks[2], (DEPTH, DEC_BATCH, WINDOW, KV_HEADS, HEAD_DIM), 1.0),
        "cache_attn_v": nrm(ks[3], (DEPTH, DEC_BATCH, WINDOW, KV_HEADS, HEAD_DIM), 1.0),
        "state_ret": nrm(ks[4], (DEPTH, DEC_BATCH, RET_HEADS, RET_HEAD_DIM, RET_HEAD_DIM), 1.0),
        "attn_norm_g": 1.0 + nrm(ks[5], (DEPTH, D_MODEL), 0.01),
        "w_in": nrm(ks[6], (DEPTH, D_MODEL, IN_WIDTH), D_MODEL ** -0.5),
        "attn_sinks": nrm(ks[7], (DEPTH, ATTN_HEADS), 0.5),
        "ret_norm_g": 1.0 + nrm(ks[8], (DEPTH, RET_WIDTH), 0.01),
        "w_out": nrm(ks[9], (DEPTH, MIX_WIDTH, D_MODEL), MIX_WIDTH ** -0.5),
        "ffn_norm_g": 1.0 + nrm(ks[10], (DEPTH, D_MODEL), 0.01),
        "peer_w_q": nrm(ks[11], (DEPTH, D_MODEL, PEER_HEADS * PEER_QDIM), D_MODEL ** -0.5),
        "peer_sub_keys": nrm(ks[12], (DEPTH, PEER_HEADS, 2, PEER_KEYS, PEER_HALF), PEER_HALF ** -0.5),
        "peer_u": nrm(ks[13], (DEPTH, PEER_EXPERTS, D_MODEL), D_MODEL ** -0.5),
        "peer_v": nrm(ks[14], (DEPTH, PEER_EXPERTS, D_MODEL), 0.5),
        "final_norm_g": 1.0 + nrm(ks[15], (D_MODEL,), 0.01),
    }

def reference(x_prompt, x_sample, cache_attn_k, cache_attn_v, state_ret, attn_norm_g, w_in, attn_sinks,
              ret_norm_g, w_out, ffn_norm_g, peer_w_q, peer_sub_keys, peer_u, peer_v, final_norm_g):
    yp, ys = x_prompt, x_sample
    bp = x_prompt.shape[0]
    kps, vps, sps, kss, vss, sss = [], [], [], [], [], []
    for l in range(DEPTH):
        params = (attn_norm_g[l], w_in[l], attn_sinks[l], ret_norm_g[l], w_out[l], ffn_norm_g[l],
                  peer_w_q[l], peer_sub_keys[l], peer_u[l], peer_v[l])
        zero_k = jnp.zeros((bp, WINDOW, KV_HEADS, HEAD_DIM), x_prompt.dtype)
        zero_s = jnp.zeros((bp, RET_HEADS, RET_HEAD_DIM, RET_HEAD_DIM), x_prompt.dtype)
        yp, kp, vp, sp = trunk_layer(yp, zero_k, zero_k, zero_s, 0, *params)
        ys, k_s, v_s, s_s = trunk_layer(ys, cache_attn_k[l], cache_attn_v[l], state_ret[l], PAST_LEN, *params)
        kps.append(kp); vps.append(vp); sps.append(sp)
        kss.append(k_s); vss.append(v_s); sss.append(s_s)
    y_prompt = rms_norm(yp, final_norm_g)
    y_sample = rms_norm(ys, final_norm_g)
    return (y_prompt, y_sample, jnp.stack(kps), jnp.stack(vps), jnp.stack(sps),
            jnp.stack(kss), jnp.stack(vss), jnp.stack(sss))


_drawn_inputs = setup_inputs


def setup_inputs(seed=0):
    import zlib

    import numpy as np

    out = dict(_drawn_inputs(seed))
    spreads = {}
    factors = {'attn_sinks': 77.236, 'ret_norm_g': 55.908, 'final_norm_g': 187.697, 'ffn_norm_g': 20.294}
    for name, (base, spread) in spreads.items():
        noise = np.random.default_rng([zlib.crc32(name.encode()), seed]).standard_normal(out[name].shape)
        drawn = base * np.exp(spread * noise) if base else spread * noise
        out[name] = __import__('jax').numpy.asarray(drawn.astype(out[name].dtype))
    for name, factor in factors.items():
        out[name] = (out[name] * factor).astype(out[name].dtype)
    return out
```

```python
from contextlib import ExitStack

import numpy as np

import concourse.bass as bass
from concourse import mybir

ALU = mybir.AluOpType
ACT = mybir.ActivationFunctionType
F32 = mybir.dt.float32
I32 = mybir.dt.int32
U32 = mybir.dt.uint32
AX_X = mybir.AxisListType.X

P = 128
D = 1024
KC = D // P
CHUNK = 64
WINDOW = 128
HD = 64
HEADS = 8
KVH = 2
RH = 8
AW = HEADS * HD
KVW = KVH * HD
RW = RH * HD
IN_W = AW + 2 * KVW + 4 * RW
C_KA, C_VA = AW, AW + KVW
C_QR = AW + 2 * KVW
C_KR, C_VR, C_GT = C_QR + RW, C_QR + 2 * RW, C_QR + 3 * RW
PH = 8
NKEY = 128
TOPK = 16
HC = 2 * PH
EPS = 1e-6
SLOTS = PH * TOPK
PROMPT_BLOCKS = 8
NBLK = PROMPT_BLOCKS + 1
SAMPLE = PROMPT_BLOCKS
MASKED_DIST = 1e30 * 256

WCOLS = 256
N_IN, N_OUT, N_Q = IN_W // WCOLS, D // WCOLS, 2 * PH * 128 // WCOLS
PIECES = N_IN + N_OUT + N_Q
WRING = 3
WORK = 9216
RING = 8

SLOPES = [2.0 ** (-8.0 * (h + 1) / HEADS) for h in range(HEADS)]


def rows(b):
    return CHUNK if b == SAMPLE else P


def u_slots(b):
    return SLOTS // 2 if b == SAMPLE else SLOTS


def u_before(b):
    return SLOTS * b


def v_before(b):
    return P * b


def v_token(b, i):
    groups = rows(b) // 32
    return 32 * (i % groups) + i // groups


PHASES = [
    ([0], []),
    ([1, 2], [(0, None), (None, 0)]),
    ([3, 4], [(1, None), (2, 1)]),
    ([5, 6], [(3, 2), (4, 3)]),
    ([7, 8], [(5, 4), (6, 5)]),
    ([], [(7, 6), (8, 7), (None, 8)]),
]


def gather_order():
    order = {}
    for _, segs in PHASES:
        for u, v in segs:
            for k in range(seg_len((u, v))):
                if u is not None and k < u_slots(u):
                    order["u", u_before(u) + k] = len(order)
                if v is not None and k < rows(v):
                    order["v", v_before(v) + k] = len(order)
    return order


def seg_len(seg):
    u, v = seg
    return max(u_slots(u) if u is not None else 0, rows(v) if v is not None else 0)


class Pace:

    NORM, PIECE, ATTN, PEER = 4, 3.5, 30, 55

    def __init__(self, blocks, segs):
        g = len(blocks)
        self.g = g
        self.slots = sum(seg_len(s) for s in segs)
        at, self.base = 0.0, {}
        for name, width in (("norm1", g * self.NORM), ("w_in", g * N_IN * self.PIECE), ("attn", g * self.ATTN),
                            ("w_out", g * N_OUT * self.PIECE), ("norm2", g * self.NORM),
                            ("w_q", g * N_Q * self.PIECE), ("peer", g * self.PEER)):
            self.base[name] = at
            at += width
        self.total = at
        self.width = {"norm1": self.NORM, "norm2": self.NORM, "attn": self.ATTN, "peer": self.PEER,
                      "w_in": self.PIECE, "w_out": self.PIECE, "w_q": self.PIECE}

    def slot(self, step, n, part=0.0):
        at = self.base[step] + self.width[step] * (n + part)
        return int(at / self.total * (self.slots - 6)) if self.slots else 0


def shape_constants():
    q = np.arange(P)
    k = np.arange(-WINDOW, P)
    qc, kc = q // CHUNK, k // CHUNK
    valid = (kc[None, :] <= qc[:, None]) & (kc[None, :] >= qc[:, None] - WINDOW // CHUNK)
    dist = np.where(valid, np.abs(q[:, None] - k[None, :]), MASKED_DIST).astype(np.float32)
    lg = np.log(1.0 - 2.0 ** (-5.0 - np.arange(RH))).astype(np.float32).astype(np.float64)
    scale = HD ** -0.5
    j, i = np.arange(P)[:, None], np.arange(P)[None, :]
    seen = (j // CHUNK) <= (i // CHUNK)
    decay = np.zeros((P, 2, RH // 2, P))
    gin = np.zeros((P, RH // 2, P))
    gout = np.zeros((P, 2, RH))
    gblk = np.zeros((P, 2, RH // 2))
    for h in range(RH):
        g = np.exp(lg[h])
        decay[:, h % 2, h // 2] = np.where(seen, g ** np.abs(i - j), 0.0) * scale
        half = slice(HD * (h % 2), HD * (h % 2) + HD)
        gin[half, h // 2] = g ** (np.arange(P) + 1.0)
        gout[:, 0, h] = g ** (P - 1.0 - np.arange(P)) * scale
        gout[:CHUNK, 1, h] = g ** (CHUNK - 1.0 - np.arange(CHUNK)) * scale
        gblk[half, 0, h // 2] = g ** P
        gblk[half, 1, h // 2] = g ** CHUNK
    iota = np.tile(np.arange(TOPK), (P, 1))
    parts = [dist, decay.reshape(P, -1), gin.reshape(P, -1), gout.reshape(P, -1), gblk.reshape(P, -1),
             iota, np.eye(P)]
    return np.concatenate([a.astype(np.float32) for a in parts], axis=1)


CONST_WIDTHS = [WINDOW + P, RH * P, RH // 2 * P, 2 * RH, RH, TOPK, P]


def hymba_peer_program(nc, x_prompt, x_sample, cache_attn_k, cache_attn_v, state_ret, attn_norm_g, w_in,
                       attn_sinks, ret_norm_g, w_out, ffn_norm_g, peer_w_q, peer_sub_keys, peer_u, peer_v,
                       final_norm_g, tables, y_prompt, y_sample, new_k_prompt, new_v_prompt, new_s_prompt,
                       new_k_sample, new_v_sample, new_s_sample):
    u_table, v_table = peer_u[0], peer_v[0]
    w_views = [w[0].rearrange("(k p) n -> p k n", p=P) for w in (w_in, w_out, peer_w_q)]

    def w_piece(n):
        if n < N_IN:
            view, n = w_views[0], n
        elif n < N_IN + N_OUT:
            view, n = w_views[1], n - N_IN
        else:
            view, n = w_views[2], n - N_IN - N_OUT
        return view[:, :, n * WCOLS:(n + 1) * WCOLS]

    def x_rows(b):
        return x_sample[0] if b == SAMPLE else x_prompt[0, b * P:(b + 1) * P, :]

    def y_rows(b):
        return y_sample[0] if b == SAMPLE else y_prompt[0, b * P:(b + 1) * P, :]

    x1_dram = nc.dram_tensor("x1_scratch", (NBLK, P, D), F32).ap()
    h2_dram = nc.dram_tensor("h2_scratch", (NBLK, P, D), F32).ap()
    expert_dram = nc.dram_tensor("expert_scratch", (NBLK, P, SLOTS), I32).ap()
    expertT_dram = nc.dram_tensor("expertT_scratch", (NBLK, SLOTS, P), I32).ap()
    gate_dram = nc.dram_tensor("gate_scratch", (NBLK, P, SLOTS), F32).ap()

    with ExitStack() as ctx:
        def sb(name, shape, dt=F32):
            return ctx.enter_context(nc.sbuf_tensor(name, shape, dt))

        def sem(name):
            return ctx.enter_context(nc.semaphore(name))

        const = sb("const", [P, sum(CONST_WIDTHS)])
        ends = np.cumsum(CONST_WIDTHS).tolist()
        cv = [const[:, e - w:e] for e, w in zip(ends, CONST_WIDTHS)]
        dist, ident, iota16 = cv[0], cv[6], cv[5]
        decay = cv[1].rearrange("p (e a i) -> p e a i", e=2, a=RH // 2)
        gin = cv[2].rearrange("p (a i) -> p a i", i=P)
        gout = cv[3].rearrange("p (s h) -> p s h", s=2)
        gblk = cv[4].rearrange("p (s a) -> p s a", s=2)

        g_attn = sb("g_attn", [P, D])
        g_ffn = sb("g_ffn", [P, D])
        g_fin = sb("g_fin", [P, D])
        g_ret = sb("g_ret", [P, RW])
        sinks = sb("sinks", [P, HEADS])
        wbuf = sb("wbuf", [P, WRING, KC, WCOLS])
        keysT = sb("keysT", [P, HC, NKEY])
        x_in = sb("x_in", [P, 2, D])
        h_nat = sb("h_nat", [P, D])
        actT = sb("actT", [P, 2, KC, P])
        wide = sb("wide", [P, 2 * IN_W])
        proj = [wide[:, g * IN_W:(g + 1) * IN_W] for g in range(2)]
        pq = [wide[:, g * HC * P:(g + 1) * HC * P] for g in range(2)]
        work = sb("work", [P, WORK])
        off = [0]

        def part(n):
            off[0] += n
            assert off[0] <= WORK
            return work[:, off[0] - n:off[0]]

        KW = WINDOW + P
        scores = part(HEADS * KW).rearrange("p (h k) -> p h k", h=HEADS)
        probsT = part(HEADS * KW).rearrange("p (h s q) -> p h s q", h=HEADS, s=2)
        qT = part(AW).rearrange("p (j q) -> p j q", q=P)
        qrT = part(RW).rearrange("p (a q) -> p a q", q=P)
        krT = part(RW).rearrange("p (a q) -> p a q", q=P)
        qrTs = part(RW).rearrange("p (a q) -> p a q", q=P)
        retP = part(RH * P).rearrange("p (e a i) -> p e a i", e=2, a=RH // 2)
        k_dec = part(RW)
        centred = part(RW)
        squares = part(RW)
        gate_e = part(RW)
        off[0] = 0
        pqT = part(HC * P).rearrange("p (c t) -> p c t", t=P)
        sims = part(HC * NKEY).rearrange("p (c n) -> p c n", n=NKEY)
        cand = part(PH * TOPK * TOPK).rearrange("p (h n) -> p h n", h=PH)
        onehot = part(PH * TOPK * TOPK).rearrange("p (h k i) -> p h k i", h=PH, k=TOPK)
        top_f = part(HC * TOPK).rearrange("p (c k) -> p c k", k=TOPK)
        pos_f = part(2 * SLOTS).rearrange("p (s n) -> p s n", s=2)
        half_f = part(2 * SLOTS).rearrange("p (s n) -> p s n", s=2)
        expert_f = part(SLOTS)
        off[0] = 0
        top_i = part(HC * TOPK).bitcast(U32).rearrange("p (c k) -> p c k", k=TOPK)
        best_p = part(PH * TOPK).bitcast(U32).rearrange("p (h k) -> p h k", k=TOPK)
        pos_u = part(2 * SLOTS).bitcast(U32).rearrange("p (s n) -> p s n", s=2)
        junk = work[:, 0:D]

        cache_kT = sb("cache_kT", [P, WINDOW])
        kT_win = sb("kT_win", [P, WINDOW + P])
        v_prev = sb("v_prev", [P, KVW])
        cache_k = sb("cache_k", [P, KVW])
        cache_v = sb("cache_v", [P, KVW])
        state = sb("state", [P, RH // 2, 2 * HD])
        state_s = sb("state_s", [P, RH // 2, HD])
        state_p = sb("state_p", [P, RH // 2, HD])
        stats = sb("stats", [P, 8, HEADS])
        row_max, neg_max, sink_e, den, rden, r_sum, r_var, r_std = (stats[:, i, :] for i in range(8))
        norm_s = sb("norm_s", [P, 8])
        top_v = sb("top_v", [P, HC, TOPK])
        best_v = sb("best_v", [P, PH, TOPK])
        expert_i = sb("expert_i", [P, SLOTS], I32)
        expertT_i = sb("expertT_i", [P, P], I32)
        gate_w = sb("gate_w", [P, SLOTS])
        g_stat = sb("g_stat", [P, 2, PH])

        ring = sb("ring", [P, RING, D])
        u_idx = sb("u_idx", [P, 2, SLOTS], I32)
        v_idx = sb("v_idx", [P, 2, P], I32)
        u_x = sb("u_x", [P, 2, D])
        u_gate = sb("u_gate", [P, 2, SLOTS])
        hidden = sb("hidden", [P, SLOTS])
        weight = sb("weight", [P, SLOTS])
        spread = sb("spread", [P, P * 32])
        x1_v = sb("x1_v", [P, D])
        fin_s = sb("fin_s", [P, 4])

        ps = ctx.enter_context(nc.psum_tensor("ps", [P, 8, 512], F32))
        B_WT, B_ACC = 5, 6

        consts_in = sem("consts_in")
        cache_in = sem("cache_in")
        keys_in = sem("keys_in")
        x_landed = [sem(f"x_landed{g}") for g in range(2)]
        w_landed = [sem(f"w_landed{i}") for i in range(WRING)]
        x1_stored = [sem(f"x1_stored{g}") for g in range(2)]
        h2_stored = sem("h2_stored")
        expert_stored = sem("expert_stored")
        u_in = [sem(f"u_in{i}") for i in range(2)]
        v_in = [sem(f"v_in{i}") for i in range(2)]
        x1_in = sem("x1_in")
        landed = [sem(f"landed{i}") for i in range(RING)]
        y_stored = sem("y_stored")
        side_stored = sem("side_stored")
        vec_step = sem("vec_step")
        act_step = sem("act_step")
        cleared = sem("cleared")
        keys_tr = sem("keys_tr")
        keys_ready = sem("keys_ready")
        cache_tr = sem("cache_tr")
        kv_carried = sem("kv_carried")
        sq1_ready, ms1_ready, sd1_ready = sem("sq1_ready"), sem("ms1_ready"), sem("sd1_ready")
        h_ready, h_tr, hT_ready = sem("h_ready"), sem("h_tr"), sem("hT_ready")
        in_done, proj_ready = sem("in_done"), sem("proj_ready")
        qk_tr, qk_ready = sem("qk_tr"), sem("qk_ready")
        scores_done, scores_read = sem("scores_done"), sem("scores_read")
        max_ready, exp_ready, gate_exp = sem("max_ready"), sem("exp_ready"), sem("gate_exp")
        ret_done, retP_ready = sem("ret_done"), sem("retP_ready")
        or_done, kv_done, or_read = sem("or_done"), sem("kv_done"), sem("or_read")
        state_ready = sem("state_ready")
        var_ready, sd_ready = sem("var_ready"), sem("sd_ready")
        probs_tr, probsT_ready = sem("probs_tr"), sem("probsT_ready")
        ctx_done, mixed_ready = sem("ctx_done"), sem("mixed_ready")
        mix_tr, mixT_ready = sem("mix_tr"), sem("mixT_ready")
        out_done, x1_ready = sem("out_done"), sem("x1_ready")
        sq2_ready, ms2_ready, sd2_ready = sem("sq2_ready"), sem("ms2_ready"), sem("sd2_ready")
        h2_ready, h2_tr, h2T_ready = sem("h2_ready"), sem("h2_tr"), sem("h2T_ready")
        q_done, q_ready = sem("q_done"), sem("q_ready")
        pq_tr, pqT_ready = sem("pq_tr"), sem("pqT_ready")
        sims_done, sims_ready = sem("sims_done"), sem("sims_ready")
        gdiff_ready, gexp_ready = sem("gdiff_ready"), sem("gexp_ready")
        expert_ready = sem("expert_ready")
        expert_tr, expertT_ready = sem("expert_tr"), sem("expertT_ready")
        dots_done = sem("dots_done")
        summed = sem("summed")
        gelu_ready, weight_ready, weight_tr, spread_ready = (
            sem("gelu_ready"), sem("weight_ready"), sem("weight_tr"), sem("spread_ready"))
        acc_read, fin_ms, fin_sd, y_ready = sem("acc_read"), sem("fin_ms"), sem("fin_sd"), sem("y_ready")

        block = ctx.enter_context(nc.Block())

        class Threader:

            def __init__(self, slot, end, before=None):
                self.slot, self.end, self.before = slot, end, before

            def phase(self, blocks, segs):
                self.pace = Pace(blocks, segs)
                self.todo = [(s, k) for s in segs for k in range(seg_len(s))]
                self.at = 0

            def upto(self, n):
                while self.at < min(n, len(self.todo)):
                    seg, k = self.todo[self.at]
                    if k == 0 and self.before:
                        self.before(seg)
                    self.slot(seg, k)
                    self.at += 1
                    if k == seg_len(seg) - 1:
                        self.end(seg)

            def step(self, name, n, part=0.0):
                self.upto(self.pace.slot(name, n, part))

            def rest(self):
                self.upto(len(self.todo))

        class Chain:

            def __init__(self, eng, own):
                self.eng, self.own, self.count, self.last = eng, own, {}, None

            def put(self, ins, signal=None):
                signal = signal or self.own
                ins.then_inc(signal, 1)
                self.count[signal.name] = self.count.get(signal.name, 0) + 1
                self.last = (signal, self.count[signal.name])

            def settle(self):
                self.eng.wait_ge(*self.last)

        order = gather_order()
        gathers = {n: kind for kind, n in order.items()}

        def await_tile(eng, kind, n):
            at = order[kind, n]
            eng.wait_ge(landed[at % RING], 16 * (at // RING + 1))
            return ring[:, at % RING, :]

        def nothing(*_):
            pass

        def x_buffer(b):
            return 0 if b == 0 else (b + 1) % 2

        def x1_stores(b):
            return 1 if b == 0 else (b + 3) // 2 if b % 2 else b // 2

        def u_loads(b):
            return 3 * (b // 2 + 1) + (3 if b == SAMPLE else 0)

        @block.sync
        def _(sp):
            def load_piece(blocks, n):
                b0, G = blocks[0], len(blocks)
                m = n - WRING
                if m < 0 and b0:
                    sp.wait_ge(q_done, N_Q * b0)
                elif 0 <= m < N_IN:
                    sp.wait_ge(in_done, N_IN * b0 + (m + 1) * G)
                elif N_IN <= m < N_IN + N_OUT:
                    sp.wait_ge(out_done, N_OUT * b0 + (m - N_IN + 1) * G)
                elif m >= 0:
                    sp.wait_ge(q_done, N_Q * b0 + (m - N_IN - N_OUT + 1) * G)
                sp.dma_start(wbuf[:, n % WRING], w_piece(n)).then_inc(w_landed[n % WRING], 16)

            def load_x(b):
                g = x_buffer(b)
                if b:
                    sp.wait_ge(h2_ready, b if b == 1 else 2 * ((b - 1) // 2) + 1)
                    if b != 2:
                        sp.wait_ge(x1_stored[g], 16 * (x1_stores(b) - 1))
                sp.dma_start(x_in[0:rows(b), g, :], x_rows(b)).then_inc(x_landed[g], 16)

            def load_segment(seg):
                u, v = seg
                if u is not None:
                    sp.wait_ge(h2_stored, 16 * (u + 1))
                    sp.wait_ge(expert_stored, 48 * (u + 1))
                    if u >= 2:
                        sp.wait_ge(weight_ready, u - 1)
                    i = u % 2
                    parts = [(slice(0, P), slice(0, P), slice(0, SLOTS))]
                    if u == SAMPLE:
                        parts = [(slice(64 * n, 64 * n + 64), slice(0, 64), slice(64 * n, 64 * n + 64))
                                 for n in range(2)]
                    for dst, src, cols in parts:
                        width = cols.stop - cols.start
                        sp.dma_start(u_idx[dst, i, 0:width], expert_dram[u, src, cols]).then_inc(u_in[i], 16)
                        sp.dma_start(u_gate[dst, i, 0:width], gate_dram[u, src, cols]).then_inc(u_in[i], 16)
                        sp.dma_start(u_x[dst, i, :], h2_dram[u, src, :]).then_inc(u_in[i], 16)
                if v is not None:
                    if v >= 2:
                        sp.wait_ge(summed, v_before(v - 1))
                    sp.dma_start(v_idx[:, v % 2, 0:rows(v)], expertT_dram[v, :, 0:rows(v)]
                                 ).then_inc(v_in[v % 2], 16)

            def store_window_and_state(b, g):
                T = rows(b)
                sp.wait_ge(proj_ready, N_IN * NBLK)
                for c, old, dst_p, dst_s in ((C_KA, cache_k, new_k_prompt, new_k_sample),
                                             (C_VA, cache_v, new_v_prompt, new_v_sample)):
                    dst = (dst_s if b == SAMPLE else dst_p)[0, 0].rearrange("t h d -> t (h d)")
                    sp.dma_start(dst[WINDOW - T:WINDOW, :], proj[g][0:T, c:c + KVW]).then_inc(side_stored, 16)
                    if b == SAMPLE:
                        sp.wait_ge(cache_in, 64)
                        sp.dma_start(dst[0:WINDOW - T, :], old[T:WINDOW, :]).then_inc(side_stored, 16)
                sp.wait_ge(state_ready, b + 1)
                dst = (new_s_sample if b == SAMPLE else new_s_prompt)[0, 0].rearrange("(a e) d f -> e d a f", e=2)
                for e in range(2):
                    half = slice(HD * e, HD * e + HD)
                    src = state[half, :, half] if b == SAMPLE else state_p[half, :, :]
                    sp.dma_start(dst[e], src).then_inc(side_stored, 16)

            th = Threader(nothing, nothing, load_segment)
            for blocks, segs in PHASES:
                th.phase(blocks, segs)
                th.upto(1)
                G = len(blocks)
                if not G:
                    th.rest()
                    continue
                b0 = blocks[0]
                if b0 == 0:
                    load_x(0)
                    sp.dma_start(const[:], tables).then_inc(consts_in, 16)
                    for t, src in ((g_attn, attn_norm_g[0]), (g_ffn, ffn_norm_g[0]), (g_ret, ret_norm_g[0]),
                                   (sinks, attn_sinks[0]), (g_fin, final_norm_g)):
                        sp.dma_start(t[:], src.partition_broadcast(P)).then_inc(consts_in, 16)
                    sp.dma_start(sims[:, :, :], peer_sub_keys[0].rearrange("h c n d -> n (h c) d")
                                 ).then_inc(keys_in, 16)
                    sp.dma_start(cache_k[:], cache_attn_k[0, 0].rearrange("t h d -> t (h d)")).then_inc(cache_in, 16)
                    sp.dma_start(cache_v[:], cache_attn_v[0, 0].rearrange("t h d -> t (h d)")).then_inc(cache_in, 16)
                    old = state_ret[0, 0].rearrange("(a e) d f -> e d a f", e=2)
                    for e in range(2):
                        half = slice(HD * e, HD * e + HD)
                        sp.dma_start(state_s[half, :, :], old[e]).then_inc(cache_in, 16)
                for n in range(WRING):
                    load_piece(blocks, n)
                if b0:
                    for b in blocks:
                        load_x(b)
                for n in range(WRING, PIECES):
                    m = n - WRING
                    name, first = (("w_in", 0) if m < N_IN else ("w_out", N_IN) if m < N_IN + N_OUT
                                   else ("w_q", N_IN + N_OUT))
                    if m == N_IN:
                        for g, b in enumerate(blocks):
                            if b >= SAMPLE - 1:
                                th.step("attn", g, 1.0)
                                store_window_and_state(b, g)
                    if m == N_IN + N_OUT:
                        for g, b in enumerate(blocks):
                            th.step("norm2", g)
                            T = rows(b)
                            sp.wait_ge(x1_ready, N_OUT * b0 + (N_OUT - 1) * G + g + 1)
                            sp.dma_start(x1_dram[b, 0:T, :], x_in[0:T, g, :]).then_inc(x1_stored[g], 16)
                            sp.wait_ge(h2_ready, b + 1)
                            sp.dma_start(h2_dram[b, 0:T, :], h_nat[0:T, :]).then_inc(h2_stored, 16)
                    th.step(name, (m - first) * G + G - 1, 0.5)
                    load_piece(blocks, n)
                for g, b in enumerate(blocks):
                    th.step("peer", g, 0.98)
                    T = rows(b)
                    sp.wait_ge(expert_ready, 2 * b + 2)
                    sp.dma_start(expert_dram[b, 0:T, :], expert_i[0:T, :]).then_inc(expert_stored, 16)
                    sp.dma_start(gate_dram[b, 0:T, :], gate_w[0:T, :]).then_inc(expert_stored, 16)
                    sp.wait_ge(expertT_ready, b + 1)
                    sp.dma_start(expertT_dram[b, :, 0:T], expertT_i[:, 0:T]).then_inc(expert_stored, 16)
                th.rest()
            sp.wait_ge(y_stored, 16 * NBLK)
            sp.wait_ge(side_stored, 16 * 10)
            for g in range(2):
                sp.wait_ge(x1_stored[g], 16 * x1_stores(PROMPT_BLOCKS - 1 + g))
            sp.wait_ge(h2_stored, 16 * NBLK)
            sp.wait_ge(expert_stored, 48 * NBLK)

        @block.gpsimd
        def _(pool):
            pool.memset(spread[:], 0.0).then_inc(cleared, 1)
            pool.memset(weight[:], 0.0).then_inc(cleared, 1)
            pool.memset(state[:, :, :], 0.0).then_inc(cleared, 1)

            def gather(at, table, idx):
                if at >= RING:
                    kind, n = gathers[at - RING]
                    pool.wait_ge(dots_done if kind == "u" else summed, n + 1)
                pool.indirect_dma_start(ring[:, at % RING, :], None, table,
                                        bass.IndirectOffsetOnAxis(ap=idx, axis=0)).then_inc(landed[at % RING], 16)

            def slot(seg, k):
                u, v = seg
                if u is not None and k < u_slots(u):
                    i, n = u % 2, u_before(u) + k
                    if k == 0:
                        pool.wait_ge(u_in[i], 16 * u_loads(u))
                    gather(order["u", n], u_table, u_idx[:, i, k:k + 1])
                if v is not None and k < rows(v):
                    i, n, t = v % 2, v_before(v) + k, v_token(v, k)
                    if k == 0:
                        pool.wait_ge(v_in[i], 16 * (v // 2 + 1))
                    gather(order["v", n], v_table, v_idx[:, i, t:t + 1])

            th = Threader(slot, nothing)
            for blocks, segs in PHASES:
                th.phase(blocks, segs)
                th.rest()

        @block.scalar
        def _(act):
            ch = Chain(act, act_step)
            copy = nc.scalar.copy

            def load_x1(seg):
                v = seg[1]
                if v is not None:
                    g = x_buffer(v)
                    act.wait_ge(x1_stored[g], 16 * x1_stores(v))
                    if v:
                        act.wait_ge(y_stored, 16 * v)
                    act.dma_start(x1_v[0:rows(v), :], x1_dram[v, 0:rows(v), :]).then_inc(x1_in, 16)

            def end(seg):
                u, v = seg
                if u is not None:
                    n = u_slots(u)
                    act.wait_ge(dots_done, u_before(u) + n)
                    ch.put(nc.scalar.activation(hidden[:, 0:n], hidden[:, 0:n], ACT.Gelu), gelu_ready)
                if v is not None:
                    T = rows(v)
                    act.wait_ge(fin_ms, v + 1)
                    ch.put(nc.scalar.activation(fin_s[0:T, 2:3], fin_s[0:T, 1:2], ACT.Sqrt), fin_sd)
                    act.wait_ge(y_ready, v + 1)
                    act.dma_start(y_rows(v), x1_v[0:T, :]).then_inc(y_stored, 16)

            def square_sum(b, g, landed, ms, sd, sq):
                T = rows(b)
                if ch.last:
                    ch.settle()
                ch.put(nc.scalar.activation(junk[0:T, :], x_in[0:T, g, :], ACT.Square,
                                            accum_out=norm_s[0:T, g:g + 1]), sq)
                act.wait_ge(ms, b + 1)
                ch.put(nc.scalar.activation(norm_s[0:T, 4 + g:5 + g], norm_s[0:T, 2 + g:3 + g], ACT.Sqrt), sd)

            def four(bank, T):
                return ps[:, bank, :].rearrange("p (c t) -> p c t", c=4)[:, :, 0:T]

            th = Threader(nothing, end, load_x1)
            for blocks, segs in PHASES:
                th.phase(blocks, segs)
                G = len(blocks)
                if not G:
                    th.rest()
                    continue
                b0 = blocks[0]
                for g, b in enumerate(blocks):
                    th.step("norm1", g)
                    act.wait_ge(x_landed[g], 16 * x1_stores(b))
                    if b == 0:
                        act.wait_ge(cleared, 3)
                    square_sum(b, g, None, ms1_ready, sd1_ready, sq1_ready)
                if b0 == 0:
                    for i in range(4):
                        act.wait_ge(keys_tr, i + 1)
                        ch.put(copy(keysT[:, 4 * i:4 * i + 4, :], four(i, P)), keys_ready)
                    act.wait_ge(cache_tr, 1)
                    ch.put(copy(cache_kT[:], ps[:, 4, 0:P]))
                for g, b in enumerate(blocks):
                    T = rows(b)
                    th.step("norm1", g, 0.5)
                    for i in range(2):
                        act.wait_ge(h_tr, 2 * b + i + 1)
                        ch.put(copy(actT[:, g, 4 * i:4 * i + 4, 0:T], four(i, T)), hT_ready)
                for p in range(N_IN):
                    for g, b in enumerate(blocks):
                        m = p * G + g
                        th.step("w_in", m, 0.5)
                        act.wait_ge(in_done, N_IN * b0 + m + 1)
                        T = rows(b)
                        dst, src = proj[g][0:T, p * WCOLS:(p + 1) * WCOLS], ps[0:T, 2 + m % 2, 0:WCOLS]
                        if p < KVH:
                            dst = proj[g][0:T, 0:AW].rearrange("p (j v d) -> p j v d", v=KVH, d=HD)[:, :, p, :]
                            src = src.rearrange("p (j d) -> p j d", d=HD)
                        ch.put(copy(dst, src), proj_ready)
                for g, b in enumerate(blocks):
                    T = rows(b)
                    lo, hi = (WINDOW if b == 0 else 0), WINDOW + T
                    th.step("attn", g, 0.05)
                    act.wait_ge(qk_tr, 4 * b + 1)
                    ch.put(nc.scalar.mul(qT[:, :, 0:T], four(0, T), HD ** -0.5), qk_ready)
                    act.wait_ge(qk_tr, 4 * b + 2)
                    if b:
                        ch.settle()
                    ch.put(copy(kT_win[:, WINDOW:WINDOW + T], ps[:, 1, 0:T]), qk_ready)
                    act.wait_ge(qk_tr, 4 * b + 3)
                    ch.put(copy(qrT[:, :, 0:T], four(2, T)), qk_ready)
                    act.wait_ge(qk_tr, 4 * b + 4)
                    ch.put(copy(krT[:, :, 0:T], four(3, T)), qk_ready)
                    ch.put(nc.scalar.activation(gate_e[0:T, :], proj[g][0:T, C_GT:C_GT + RW], ACT.Exp, scale=-1.0),
                           gate_exp)
                    th.step("attn", g, 0.25)
                    act.wait_ge(max_ready, b + 1)
                    for h in range(HEADS):
                        ch.put(nc.scalar.activation(scores[0:T, h, lo:hi], scores[0:T, h, lo:hi], ACT.Exp,
                                                    bias=neg_max[0:T, h:h + 1], accum_out=den[0:T, h:h + 1]))
                    ch.put(nc.scalar.activation(sink_e[0:T, :], sink_e[0:T, :], ACT.Exp), exp_ready)
                    th.step("attn", g, 0.55)
                    act.wait_ge(var_ready, b + 1)
                    ch.put(nc.scalar.activation(r_std[0:T, :], r_var[0:T, :], ACT.Sqrt), sd_ready)
                    th.step("attn", g, 0.65)
                    for i in range(4):
                        act.wait_ge(probs_tr, 4 * b + i + 1)
                        src = ps[:, i, :].rearrange("p (h s q) -> p h s q", h=2, s=2)
                        dst = probsT[:, 2 * i:2 * i + 2, :, :]
                        if b == 0:
                            ch.put(copy(dst[:, :, 1, :], src[:, :, 1, :]), probsT_ready)
                        elif b == SAMPLE:
                            ch.put(copy(dst[:, :, 0, 0:T], src[:, :, 0, 0:T]))
                            ch.put(copy(dst[0:T, :, 1, 0:T], src[0:T, :, 1, 0:T]), probsT_ready)
                        else:
                            ch.put(copy(dst, src), probsT_ready)
                    th.step("attn", g, 0.8)
                    if b < SAMPLE:
                        act.wait_ge(ctx_done, b + 1)
                        ch.settle()
                        cached = b + 1 == SAMPLE
                        if cached:
                            act.wait_ge(cache_in, 64)
                        ch.put(copy(kT_win[:, 0:WINDOW], cache_kT[:] if cached else kT_win[:, WINDOW:WINDOW + T]))
                        ch.put(copy(v_prev[:], cache_v[:] if cached else proj[g][:, C_VA:C_VA + KVW]), kv_carried)
                    th.step("attn", g, 0.9)
                    for i in range(2):
                        act.wait_ge(mix_tr, 2 * b + i + 1)
                        ch.put(copy(actT[:, g, 4 * i:4 * i + 4, 0:T], four(i, T)), mixT_ready)
                for g, b in enumerate(blocks):
                    th.step("norm2", g)
                    act.wait_ge(x1_ready, N_OUT * b0 + (N_OUT - 1) * G + g + 1)
                    square_sum(b, g, None, ms2_ready, sd2_ready, sq2_ready)
                for g, b in enumerate(blocks):
                    T = rows(b)
                    th.step("norm2", g, 0.5)
                    for i in range(2):
                        act.wait_ge(h2_tr, 2 * b + i + 1)
                        ch.put(copy(actT[:, g, 4 * i:4 * i + 4, 0:T], four(i, T)), h2T_ready)
                if blocks[-1] == SAMPLE:
                    act.wait_ge(side_stored, 16 * 10)
                for p in range(N_Q):
                    for g, b in enumerate(blocks):
                        m = p * G + g
                        th.step("w_q", m, 0.5)
                        act.wait_ge(q_done, N_Q * b0 + m + 1)
                        ch.put(copy(pq[g][0:rows(b), p * WCOLS:(p + 1) * WCOLS],
                                    ps[0:rows(b), 2 + m % 2, 0:WCOLS]), q_ready)
                for g, b in enumerate(blocks):
                    T = rows(b)
                    th.step("peer", g)
                    if b:
                        act.wait_ge(expert_ready, 2 * b)
                    for i in range(4):
                        act.wait_ge(pq_tr, 4 * b + i + 1)
                        ch.put(copy(pqT[:, 4 * i:4 * i + 4, 0:T], four(i, T)), pqT_ready)
                    for i in range(4):
                        act.wait_ge(sims_done, 4 * b + i + 1)
                        ch.put(copy(sims[0:T, 4 * i:4 * i + 4, :], four(i, P)[0:T]), sims_ready)
                    th.step("peer", g, 0.85)
                    act.wait_ge(gdiff_ready, b + 1)
                    ch.put(nc.scalar.activation(best_v[0:T, :, :], best_v[0:T, :, :], ACT.Exp), gexp_ready)
                th.rest()

        @block.vector
        def _(dve):
            ch = Chain(dve, vec_step)
            v_ = nc.vector

            def slot(seg, k):
                u = seg[0]
                if u is None or k >= u_slots(u):
                    return
                i, n = u % 2, u_before(u) + k
                if k == 0:
                    dve.wait_ge(u_in[i], 16 * u_loads(u))
                row = await_tile(dve, "u", n)
                ch.put(v_.tensor_tensor_reduce(out=row, in0=row, in1=u_x[:, i, :], scale=1.0, scalar=0.0,
                                               op0=ALU.mult, op1=ALU.add, accum_out=hidden[:, k:k + 1]), dots_done)

            def end(seg):
                u, v = seg
                if v is not None:
                    T = rows(v)
                    dve.wait_ge(summed, v_before(v) + T)
                    dve.wait_ge(x1_in, 16 * (v + 1))
                    acc = ps[0:T, B_ACC:B_ACC + 2, :].rearrange("p a n -> p (a n)")
                    ch.put(v_.tensor_tensor(x1_v[0:T, :], x1_v[0:T, :], acc, ALU.add))
                    ch.settle()
                    ch.put(v_.tensor_tensor_reduce(out=acc, in0=x1_v[0:T, :], in1=x1_v[0:T, :], scale=1.0,
                                                   scalar=0.0, op0=ALU.mult, op1=ALU.add,
                                                   accum_out=fin_s[0:T, 0:1]), acc_read)
                if u is not None:
                    i = u % 2
                    dve.wait_ge(gelu_ready, u + 1)
                    dve.wait_ge(cleared, 3)
                    if u:
                        dve.wait_ge(weight_tr, u)
                    if u != SAMPLE:
                        ch.put(v_.tensor_tensor(weight[:], hidden[:], u_gate[:, i, :], ALU.mult), weight_ready)
                    else:
                        ch.put(v_.memset(weight[:], 0.0))
                        ch.settle()
                        for half in (slice(0, 64), slice(64, 128)):
                            w = v_.tensor_tensor(weight[half, half], hidden[half, 0:64], u_gate[half, i, 0:64],
                                                 ALU.mult)
                        ch.put(w, weight_ready)
                    dve.wait_ge(weight_tr, u + 1)
                    if u:
                        dve.wait_ge(summed, v_before(u))
                    if u != SAMPLE:
                        dst = spread[:].rearrange("p (j c) -> p j c", j=4)[:, :, 0:1024:33]
                        ch.put(v_.tensor_copy(dst, ps[:, B_WT, 0:P].rearrange("p (j r) -> p j r", j=4)),
                               spread_ready)
                    else:
                        for half in (slice(0, 64), slice(64, 128)):
                            dst = spread[half, 0:2048].rearrange("p (j c) -> p j c", j=2)[:, :, 0:1024:33]
                            w = v_.tensor_copy(dst, ps[half, B_WT, half].rearrange("p (j r) -> p j r", j=2))
                        ch.put(w, spread_ready)
                if v is not None:
                    T = rows(v)
                    ch.settle()
                    ch.put(v_.tensor_scalar(fin_s[0:T, 1:2], fin_s[0:T, 0:1], 1.0 / D, EPS, ALU.mult, ALU.add), fin_ms)
                    dve.wait_ge(fin_sd, v + 1)
                    ch.put(v_.reciprocal(fin_s[0:T, 3:4], fin_s[0:T, 2:3]))
                    ch.settle()
                    ch.put(v_.scalar_tensor_tensor(out=x1_v[0:T, :], in0=x1_v[0:T, :], scalar=fin_s[0:T, 3:4],
                                                   in1=g_fin[0:T, :], op0=ALU.mult, op1=ALU.mult), y_ready)

            def norm(b, g, sq, ms, sd, gain, out_sem):
                T = rows(b)
                dve.wait_ge(sq, b + 1)
                ch.put(v_.tensor_scalar(norm_s[0:T, 2 + g:3 + g], norm_s[0:T, g:g + 1], 1.0 / D, EPS,
                                        ALU.mult, ALU.add), ms)
                dve.wait_ge(sd, b + 1)
                ch.put(v_.reciprocal(norm_s[0:T, 6 + g:7 + g], norm_s[0:T, 4 + g:5 + g]))
                ch.settle()

                def last():
                    ch.put(v_.scalar_tensor_tensor(out=h_nat[0:T, :], in0=x_in[0:T, g, :],
                                                   scalar=norm_s[0:T, 6 + g:7 + g], in1=gain[0:T, :],
                                                   op0=ALU.mult, op1=ALU.mult), out_sem)
                return last

            def per_head(ap, T, n):
                return ap[0:T, :].unsqueeze(2).broadcast_to([T, HEADS, n])

            def top16(values, best, where, T, count, tick):
                for half in range(2):
                    out = slice(8 * half, 8 * half + 8)
                    ch.settle()
                    for c in range(count):
                        ch.put(v_.max(best[0:T, c, out], values[0:T, c, :]))
                        tick()
                    ch.settle()
                    for c in range(count):
                        ch.put(v_.max_index(where[0:T, c, out], best[0:T, c, out], values[0:T, c, :]))
                        tick()
                    if half == 0:
                        ch.settle()
                        for c in range(count):
                            ch.put(v_.match_replace(values[0:T, c, :], best[0:T, c, out], values[0:T, c, :], -3.0e38))
                            tick()

            th = Threader(slot, end)
            dve.wait_ge(consts_in, 16 * 6)
            for blocks, segs in PHASES:
                th.phase(blocks, segs)
                G = len(blocks)
                if not G:
                    th.rest()
                    continue
                b0 = blocks[0]
                for g, b in enumerate(blocks):
                    th.step("norm1", g)
                    last = norm(b, g, sq1_ready, ms1_ready, sd1_ready, g_attn, h_ready)
                    if b:
                        dve.wait_ge(h_tr, 2 * b)
                        dve.wait_ge(h2_tr, 2 * b0)
                        dve.wait_ge(h2_stored, 16 * b0)
                    last()
                for g, b in enumerate(blocks):
                    T = rows(b)
                    lo, hi = (WINDOW if b == 0 else 0), WINDOW + T
                    th.step("attn", g, 0.1)
                    dve.wait_ge(proj_ready, N_IN * b0 + (N_IN - 1) * G + g + 1)
                    ch.put(v_.tensor_tensor(k_dec[0:T, :].rearrange("p (h d) -> p h d", h=RH),
                                            proj[g][0:T, C_KR:C_KR + RW].rearrange("p (h d) -> p h d", h=RH),
                                            per_head(gout[:, 1 if b == SAMPLE else 0, :], T, HD), ALU.mult))
                    dve.wait_ge(qk_ready, 4 * b + 4)
                    ch.put(v_.tensor_tensor(qrTs[:, :, 0:T], qrT[:, :, 0:T], gin[:, :, 0:T], ALU.mult))
                    th.step("attn", g, 0.2)
                    for h in range(HEADS):
                        if h % 2 == 0:
                            dve.wait_ge(scores_done, 4 * b + h // 2 + 1)
                        c = (h % 2) * KW
                        ch.put(v_.scalar_tensor_tensor(out=scores[0:T, h, lo:hi], in0=dist[0:T, lo:hi],
                                                       scalar=-SLOPES[h], in1=ps[0:T, h // 2, c + lo:c + hi],
                                                       op0=ALU.mult, op1=ALU.add), scores_read if h % 2 else None)
                    ch.settle()
                    ch.put(v_.tensor_reduce(row_max[0:T, :], scores[0:T, :, lo:hi], AX_X, ALU.max))
                    ch.settle()
                    ch.put(v_.tensor_tensor(row_max[0:T, :], row_max[0:T, :], sinks[0:T, :], ALU.max))
                    ch.settle()
                    ch.put(v_.tensor_tensor(sink_e[0:T, :], sinks[0:T, :], row_max[0:T, :], ALU.subtract))
                    ch.put(v_.tensor_scalar(neg_max[0:T, :], row_max[0:T, :], -1.0, None, ALU.mult), max_ready)
                    th.step("attn", g, 0.35)
                    for e in range(2):
                        dve.wait_ge(ret_done, 2 * b + e + 1)
                        src = ps[0:T, e, :].rearrange("p (a i) -> p a i", i=P)[:, :, 0:T]
                        ch.put(v_.tensor_tensor(retP[0:T, e, :, 0:T], src, decay[0:T, e, :, 0:T], ALU.mult), retP_ready)
                    th.step("attn", g, 0.5)
                    dve.wait_ge(or_done, b + 1)
                    o_ps = ps[0:T, 2, :].rearrange("p (h d) -> p h d", h=RH)
                    cen = centred[0:T, :].rearrange("p (h d) -> p h d", h=RH)
                    sq = squares[0:T, :].rearrange("p (h d) -> p h d", h=RH)
                    ch.put(v_.tensor_reduce(r_sum[0:T, :], o_ps, AX_X, ALU.add))
                    ch.settle()
                    ch.put(v_.tensor_scalar(r_sum[0:T, :], r_sum[0:T, :], 1.0 / HD, None, ALU.mult))
                    ch.settle()
                    ch.put(v_.tensor_tensor(cen, o_ps, per_head(r_sum, T, HD), ALU.subtract), or_read)
                    ch.settle()
                    ch.put(v_.tensor_tensor(sq, cen, cen, ALU.mult))
                    ch.settle()
                    ch.put(v_.tensor_reduce(r_var[0:T, :], sq, AX_X, ALU.add))
                    ch.settle()
                    ch.put(v_.tensor_scalar(r_var[0:T, :], r_var[0:T, :], 1.0 / HD, EPS, ALU.mult, ALU.add), var_ready)
                    dve.wait_ge(kv_done, b + 1)
                    for e in range(2):
                        half = slice(HD * e, HD * e + HD)
                        ch.put(v_.tensor_tensor(
                            state[half, :, half], state[half, :, half],
                            gblk[half, 1 if b == SAMPLE else 0, :].unsqueeze(2).broadcast_to([HD, RH // 2, HD]),
                            ALU.mult))
                    ch.settle()
                    last_prompt = b + 1 == SAMPLE
                    for e in range(2):
                        half = slice(HD * e, HD * e + HD)
                        kv = ps[half, 3, :].rearrange("p (a f) -> p a f", a=RH // 2)[:, :, half]
                        dst = state_p[half, :, :] if last_prompt else state[half, :, half]
                        ch.put(v_.tensor_tensor(dst, state[half, :, half], kv, ALU.add),
                               state_ready if e and not last_prompt else None)
                    if last_prompt:
                        dve.wait_ge(cache_in, 64)
                        ch.settle()
                        for e in range(2):
                            half = slice(HD * e, HD * e + HD)
                            ch.put(v_.tensor_copy(state[half, :, half], state_s[half, :, :]),
                                   state_ready if e else None)
                    th.step("attn", g, 0.7)
                    dve.wait_ge(gate_exp, b + 1)
                    ch.put(v_.tensor_scalar(gate_e[0:T, :], gate_e[0:T, :], 1.0, None, ALU.add))
                    ch.settle()
                    ch.put(v_.reciprocal(gate_e[0:T, :], gate_e[0:T, :]))
                    ch.settle()
                    ch.put(v_.tensor_tensor(gate_e[0:T, :], gate_e[0:T, :], proj[g][0:T, C_GT:C_GT + RW], ALU.mult))
                    dve.wait_ge(sd_ready, b + 1)
                    ch.put(v_.reciprocal(r_std[0:T, :], r_std[0:T, :]))
                    ch.settle()
                    ch.put(v_.tensor_tensor(gate_e[0:T, :], gate_e[0:T, :], g_ret[0:T, :], ALU.mult))
                    ch.put(v_.tensor_tensor(cen, cen, per_head(r_std, T, HD), ALU.mult))
                    ch.settle()
                    dve.wait_ge(h_tr, 2 * (b0 + G))
                    if g:
                        dve.wait_ge(mix_tr, 2 * b)
                    ch.put(v_.tensor_tensor(h_nat[0:T, AW:AW + RW], centred[0:T, :], gate_e[0:T, :], ALU.mult))
                    dve.wait_ge(exp_ready, b + 1)
                    ch.put(v_.tensor_tensor(den[0:T, :], den[0:T, :], sink_e[0:T, :], ALU.add))
                    ch.settle()
                    ch.put(v_.reciprocal(rden[0:T, :], den[0:T, :]))
                    ch.settle()
                    th.step("attn", g, 0.85)
                    dve.wait_ge(ctx_done, b + 1)
                    ch.put(v_.tensor_tensor(h_nat[0:T, 0:AW].rearrange("p (h d) -> p h d", h=HEADS),
                                            ps[0:T, 4, :].rearrange("p (h d) -> p h d", h=HEADS),
                                            per_head(rden, T, HD), ALU.mult), mixed_ready)
                for p in range(N_OUT):
                    for g, b in enumerate(blocks):
                        m = p * G + g
                        th.step("w_out", m, 0.5)
                        T = rows(b)
                        dve.wait_ge(out_done, N_OUT * b0 + m + 1)
                        x = x_in[0:T, g, p * WCOLS:(p + 1) * WCOLS]
                        ch.put(v_.tensor_tensor(x, x, ps[0:T, 2 + m % 2, 0:WCOLS], ALU.add), x1_ready)
                for g, b in enumerate(blocks):
                    th.step("norm2", g)
                    last = norm(b, g, sq2_ready, ms2_ready, sd2_ready, g_ffn, h2_ready)
                    dve.wait_ge(mix_tr, 2 * (b0 + G))
                    if g:
                        dve.wait_ge(h2_tr, 2 * b)
                        dve.wait_ge(h2_stored, 16 * b)
                    last()
                for g, b in enumerate(blocks):
                    T = rows(b)
                    th.step("peer", g, 0.1)
                    ticks = [0]

                    def tick():
                        ticks[0] += 1
                        if ticks[0] % 4 == 0:
                            th.step("peer", g, 0.1 + 0.6 * ticks[0] / (5 * (HC + PH)))

                    dve.wait_ge(sims_ready, 4 * b + 4)
                    top16(sims, top_v, top_i, T, HC, tick)
                    ch.settle()
                    ch.put(v_.tensor_copy(top_f[0:T, :, :], top_i[0:T, :, :]))
                    pair = top_v[0:T, :, :].rearrange("p (h s) k -> p h s k", s=2)
                    shape = [T, PH, TOPK, TOPK]
                    ch.put(v_.tensor_tensor(cand[0:T].rearrange("p h (i j) -> p h i j", i=TOPK),
                                            pair[:, :, 0, :].unsqueeze(3).broadcast_to(shape),
                                            pair[:, :, 1, :].unsqueeze(2).broadcast_to(shape), ALU.add))
                    if b:
                        dve.wait_ge(expert_stored, 48 * b)
                    top16(cand, best_v, best_p, T, PH, tick)
                    ch.settle()
                    bv = best_v[0:T, :, :]
                    ch.put(v_.tensor_copy(g_stat[0:T, 0, :], best_v[0:T, :, 0]))
                    flat_p = best_p[0:T, :, :].rearrange("p h k -> p (h k)")
                    ch.put(v_.tensor_scalar(pos_u[0:T, 0, :], flat_p, 4, None, ALU.logical_shift_right))
                    ch.put(v_.tensor_scalar(pos_u[0:T, 1, :], flat_p, TOPK - 1, None, ALU.bitwise_and))
                    ch.settle()
                    ch.put(v_.tensor_tensor(bv, bv, g_stat[0:T, 0, :].unsqueeze(2).broadcast_to([T, PH, TOPK]),
                                            ALU.subtract), gdiff_ready)
                    ch.put(v_.tensor_copy(pos_f[0:T, :, :], pos_u[0:T, :, :]))
                    for s in range(2):
                        th.step("peer", g, 0.75 + 0.05 * s)
                        ch.settle()
                        hot = onehot[0:T].rearrange("p h k i -> p (h k) i")
                        ch.put(v_.tensor_tensor(hot, iota16[0:T].unsqueeze(1).broadcast_to([T, SLOTS, TOPK]),
                                                pos_f[0:T, s, :].unsqueeze(2).broadcast_to([T, SLOTS, TOPK]),
                                                ALU.is_equal))
                        ch.settle()
                        num = top_f[0:T, :, :].rearrange("p (h s) k -> p h s k", s=2)[:, :, s, :]
                        ch.put(v_.tensor_tensor(onehot[0:T], onehot[0:T],
                                                num.unsqueeze(2).broadcast_to([T, PH, TOPK, TOPK]), ALU.mult))
                        ch.settle()
                        ch.put(v_.tensor_reduce(half_f[0:T, s, :], hot, AX_X, ALU.add))
                    ch.settle()
                    ch.put(v_.scalar_tensor_tensor(out=expert_f[0:T, :], in0=half_f[0:T, 0, :], scalar=float(NKEY),
                                                   in1=half_f[0:T, 1, :], op0=ALU.mult, op1=ALU.add))
                    ch.settle()
                    ch.put(v_.tensor_copy(expert_i[0:T, :], expert_f[0:T, :]), expert_ready)
                    th.step("peer", g, 0.9)
                    dve.wait_ge(gexp_ready, b + 1)
                    ch.put(v_.tensor_reduce(g_stat[0:T, 0, :], bv, AX_X, ALU.add))
                    ch.settle()
                    ch.put(v_.reciprocal(g_stat[0:T, 1, :], g_stat[0:T, 0, :]))
                    ch.settle()
                    ch.put(v_.tensor_tensor(gate_w[0:T, :].rearrange("p (h k) -> p h k", h=PH), bv,
                                            g_stat[0:T, 1, :].unsqueeze(2).broadcast_to([T, PH, TOPK]), ALU.mult),
                           expert_ready)
                    th.step("peer", g, 0.98)
                    dve.wait_ge(expert_tr, b + 1)
                    ch.put(v_.tensor_copy(expertT_i[:, 0:T], ps[:, 4, 0:T]), expertT_ready)
                th.rest()

        @block.tensor
        def _(pe):
            def slot(seg, k):
                v = seg[1]
                if v is None or k >= rows(v):
                    return
                n, t = v_before(v) + k, v_token(v, k)
                if k == 0:
                    pe.wait_ge(spread_ready, v + 1)
                    if v:
                        pe.wait_ge(acc_read, v)
                tile = await_tile(pe, "v", n)
                j = 32 * (t // 32)
                for c in range(2):
                    mm = pe.matmul(ps[j:j + 32, B_ACC + c, :], spread[:, 32 * t:32 * t + 32],
                                   tile[:, 512 * c:512 * c + 512], start=(t % 32 == 0),
                                   stop=(t % 32 == 31), skip_group_check=True)
                mm.then_inc(summed, 1)

            def end(seg):
                u = seg[0]
                if u is not None:
                    pe.wait_ge(weight_ready, u + 1)
                    if u:
                        pe.wait_ge(spread_ready, u)
                    pe.transpose(ps[:, B_WT, 0:P], weight[:], ident).then_inc(weight_tr, 1)

            def transposed(bank, T, src, count, signal, width=P):
                for c in range(count):
                    mm = pe.transpose(ps[0:width, bank, c * P:c * P + T], src(c), ident[0:T, 0:T])
                mm.then_inc(signal, 1)

            def product(name, first, p, m, g, T, signal):
                n = first + p
                pe.wait_ge(w_landed[n % WRING], 16 * (grp * len(range(n % WRING, PIECES, WRING)) + n // WRING + 1))
                for k in range(KC):
                    if k == KC // 2:
                        th.step(name, m, 0.5)
                    mm = pe.matmul(ps[0:T, 2 + m % 2, 0:WCOLS], actT[:, g, k, 0:T], wbuf[:, n % WRING, k, :],
                                   start=(k == 0), stop=(k == KC - 1))
                mm.then_inc(signal, 1)

            th = Threader(slot, end)
            pe.wait_ge(consts_in, 16 * 6)
            grp = 0
            for blocks, segs in PHASES:
                th.phase(blocks, segs)
                G = len(blocks)
                if not G:
                    th.rest()
                    continue
                b0 = blocks[0]
                if b0 == 0:
                    pe.wait_ge(keys_in, 16)
                    for i in range(4):
                        transposed(i, P, lambda c: sims[:, 4 * i + c, :], 4, keys_tr)
                    pe.wait_ge(cache_in, 64)
                    transposed(4, P, lambda c: cache_k[:], 1, cache_tr)
                    pe.wait_ge(keys_ready, 4)
                for g, b in enumerate(blocks):
                    T = rows(b)
                    th.step("norm1", g, 0.5)
                    pe.wait_ge(h_ready, b + 1)
                    if b:
                        pe.wait_ge(hT_ready, 2 * b)
                        pe.wait_ge(sims_ready, 4 * b0)
                    for i in range(2):
                        transposed(i, T, lambda c: h_nat[0:T, (4 * i + c) * P:(4 * i + c + 1) * P], 4, h_tr)
                for p in range(N_IN):
                    for g, b in enumerate(blocks):
                        m = p * G + g
                        th.step("w_in", m)
                        pe.wait_ge(hT_ready, 2 * b + 2)
                        if m >= 2:
                            pe.wait_ge(proj_ready, N_IN * b0 + m - 1)
                        product("w_in", 0, p, m, g, rows(b), in_done)
                for g, b in enumerate(blocks):
                    T = rows(b)
                    lo, hi = (WINDOW if b == 0 else 0), WINDOW + T
                    pr = proj[g]
                    th.step("attn", g)
                    pe.wait_ge(proj_ready, N_IN * (b0 + G))
                    if g:
                        pe.wait_ge(mixT_ready, 2 * b)
                    transposed(0, T, lambda c: pr[0:T, c * P:(c + 1) * P], 4, qk_tr)
                    transposed(1, T, lambda c: pr[0:T, C_KA:C_KA + KVW], 1, qk_tr)
                    transposed(2, T, lambda c: pr[0:T, C_QR + c * P:C_QR + (c + 1) * P], 4, qk_tr)
                    transposed(3, T, lambda c: pr[0:T, C_KR + c * P:C_KR + (c + 1) * P], 4, qk_tr)
                    th.step("attn", g, 0.15)
                    pe.wait_ge(qk_ready, 4 * b + 4)
                    if b:
                        pe.wait_ge(kv_carried, b)
                    for h in range(HEADS):
                        half = slice(HD * (h // 4), HD * (h // 4) + HD)
                        c = (h % 2) * KW
                        mm = pe.matmul(ps[0:T, h // 2, c + lo:c + hi], qT[half, h % 4, 0:T], kT_win[half, lo:hi],
                                       start=True, stop=True)
                        if h % 2:
                            mm.then_inc(scores_done, 1)
                    th.step("attn", g, 0.3)
                    for e in range(2):
                        pe.wait_ge(scores_read, 4 * b + e + 1)
                        half = slice(HD * e, HD * e + HD)
                        for a in range(RH // 2):
                            mm = pe.matmul(ps[0:T, e, a * P:a * P + T], krT[half, a, 0:T], qrT[half, a, 0:T],
                                           start=True, stop=True)
                        mm.then_inc(ret_done, 1)
                    th.step("attn", g, 0.45)
                    pe.wait_ge(scores_read, 4 * b + 4)
                    pe.wait_ge(retP_ready, 2 * b + 2)
                    if b:
                        pe.wait_ge(state_ready, b)
                    else:
                        pe.wait_ge(cleared, 3)
                    for a in range(RH // 2):
                        pe.matmul(ps[0:T, 2, a * P:(a + 1) * P], qrTs[:, a, 0:T], state[:, a, :],
                                  start=True, stop=False, skip_group_check=True)
                        for e in range(2):
                            h = 2 * a + e
                            mm = pe.matmul(ps[0:T, 2, h * HD:(h + 1) * HD], retP[0:T, e, a, 0:T],
                                           pr[0:T, C_VR + h * HD:C_VR + (h + 1) * HD], start=False, stop=(e == 1),
                                           skip_group_check=True)
                    mm.then_inc(or_done, 1)
                    for a in range(RH // 2):
                        mm = pe.matmul(ps[:, 3, a * P:(a + 1) * P], k_dec[0:T, a * P:(a + 1) * P],
                                       pr[0:T, C_VR + a * P:C_VR + (a + 1) * P], start=True, stop=True)
                    mm.then_inc(kv_done, 1)
                    th.step("attn", g, 0.6)
                    pe.wait_ge(exp_ready, b + 1)
                    for i in range(4):
                        if i == 2:
                            pe.wait_ge(or_read, b + 1)
                        if i == 3:
                            pe.wait_ge(state_ready, b + 1)
                        for h in (2 * i, 2 * i + 1):
                            for s in range(2):
                                keys = T if s else WINDOW
                                if b == 0 and s == 0:
                                    continue
                                c = (2 * (h % 2) + s) * P
                                mm = pe.transpose(ps[0:keys, i, c:c + T], scores[0:T, h, s * WINDOW:s * WINDOW + keys],
                                                  ident[0:T, 0:T])
                        mm.then_inc(probs_tr, 1)
                    th.step("attn", g, 0.75)
                    pe.wait_ge(probsT_ready, 4 * b + 4)
                    if b:
                        pe.wait_ge(mixed_ready, b)
                        pe.wait_ge(expertT_ready, b0)
                    for h in range(HEADS):
                        v0 = HD * (h // 4)
                        out = ps[0:T, 4, h * HD:(h + 1) * HD]
                        if b:
                            pe.matmul(out, probsT[:, h, 0, 0:T], v_prev[:, v0:v0 + HD], start=True, stop=False)
                        mm = pe.matmul(out, probsT[0:T, h, 1, 0:T], pr[0:T, C_VA + v0:C_VA + v0 + HD],
                                       start=(b == 0), stop=True)
                    mm.then_inc(ctx_done, 1)
                    th.step("attn", g, 0.9)
                    pe.wait_ge(mixed_ready, b + 1)
                    for i in range(2):
                        transposed(i, T, lambda c: h_nat[0:T, (4 * i + c) * P:(4 * i + c + 1) * P], 4, mix_tr)
                for p in range(N_OUT):
                    for g, b in enumerate(blocks):
                        m = p * G + g
                        th.step("w_out", m)
                        pe.wait_ge(mixT_ready, 2 * b + 2)
                        if m >= 2:
                            pe.wait_ge(x1_ready, N_OUT * b0 + m - 1)
                        product("w_out", N_IN, p, m, g, rows(b), out_done)
                for g, b in enumerate(blocks):
                    T = rows(b)
                    th.step("norm2", g, 0.5)
                    pe.wait_ge(h2_ready, b + 1)
                    pe.wait_ge(mixT_ready, 2 * (b0 + G))
                    if g:
                        pe.wait_ge(h2T_ready, 2 * b)
                    for i in range(2):
                        transposed(i, T, lambda c: h_nat[0:T, (4 * i + c) * P:(4 * i + c + 1) * P], 4, h2_tr)
                for p in range(N_Q):
                    for g, b in enumerate(blocks):
                        m = p * G + g
                        th.step("w_q", m)
                        pe.wait_ge(h2T_ready, 2 * b + 2)
                        if m < 2:
                            pe.wait_ge(x1_ready, N_OUT * (b0 + G))
                        else:
                            pe.wait_ge(q_ready, N_Q * b0 + m - 1)
                        product("w_q", N_IN + N_OUT, p, m, g, rows(b), q_done)
                for g, b in enumerate(blocks):
                    T = rows(b)
                    th.step("peer", g)
                    pe.wait_ge(q_ready, N_Q * (b0 + G))
                    pe.wait_ge(h2T_ready, 2 * (b0 + G))
                    if g:
                        pe.wait_ge(sims_ready, 4 * b)
                    for i in range(4):
                        transposed(i, T, lambda c: pq[g][0:T, (4 * i + c) * P:(4 * i + c + 1) * P], 4, pq_tr)
                    pe.wait_ge(pqT_ready, 4 * b + 4)
                    for c in range(HC):
                        mm = pe.matmul(ps[0:T, c // 4, (c % 4) * P:(c % 4 + 1) * P], pqT[:, c, 0:T], keysT[:, c, :],
                                       start=True, stop=True)
                        if c % 4 == 3:
                            mm.then_inc(sims_done, 1)
                    th.step("peer", g, 0.95)
                    pe.wait_ge(expert_ready, 2 * b + 1)
                    transposed(4, T, lambda c: expert_f[0:T, :], 1, expert_tr)
                th.rest()
                grp += 1


_INS = ["x_prompt", "x_sample", "cache_attn_k", "cache_attn_v", "state_ret", "attn_norm_g", "w_in", "attn_sinks",
        "ret_norm_g", "w_out", "ffn_norm_g", "peer_w_q", "peer_sub_keys", "peer_u", "peer_v", "final_norm_g"]
_OUTS = [(1, 1024, D), (1, CHUNK, D), (1, 1, WINDOW, KVH, HD), (1, 1, WINDOW, KVH, HD), (1, 1, RH, HD, HD),
         (1, 1, WINDOW, KVH, HD), (1, 1, WINDOW, KVH, HD), (1, 1, RH, HD, HD)]


def kernel(**inputs):
    import concourse.bacc as _bacc
    from concourse.bass_utils import run_bass_kernel_spmd as _run

    nc = _bacc.Bacc("TRN2", target_bir_lowering=False, num_devices=1)
    arrays, args = {}, []
    feeds = [(name, np.ascontiguousarray(inputs[name])) for name in _INS] + [("tables", shape_constants())]
    for name, a in feeds:
        arrays[f"in_{name}_dram"] = a
        args.append(nc.dram_tensor(f"in_{name}_dram", a.shape, mybir.dt.from_np(a.dtype), kind="ExternalInput").ap())
    for i, shape in enumerate(_OUTS):
        args.append(nc.dram_tensor(f"out_{i}_dram", shape, F32, kind="ExternalOutput").ap())
    hymba_peer_program(nc, *args)
    r = _run(nc, [arrays], core_ids=[0])
    return tuple(r.results[0][f"out_{i}_dram"] for i in range(len(_OUTS)))
```

```python
from contextlib import ExitStack

import numpy as np

import concourse.bass as bass
from concourse import mybir

ALU = mybir.AluOpType
ACT = mybir.ActivationFunctionType
F32 = mybir.dt.float32
I32 = mybir.dt.int32
U32 = mybir.dt.uint32
AX_X = mybir.AxisListType.X

P = 128
D = 1024
KC = D // P
CHUNK = 64
WINDOW = 128
HD = 64
HEADS = 8
KVH = 2
RH = 8
AW = HEADS * HD
KVW = KVH * HD
RW = RH * HD
IN_W = AW + 2 * KVW + 4 * RW
C_KA, C_VA = AW, AW + KVW
C_QR = AW + 2 * KVW
C_KR, C_VR, C_GT = C_QR + RW, C_QR + 2 * RW, C_QR + 3 * RW
PH = 8
NKEY = 128
TOPK = 16
HC = 2 * PH
EPS = 1e-6
SLOTS = PH * TOPK
PROMPT_BLOCKS = 8
NBLK = PROMPT_BLOCKS + 1
SAMPLE = PROMPT_BLOCKS
MASKED_DIST = 1e30 * 256

WCOLS = 256
N_IN, N_OUT, N_Q = IN_W // WCOLS, D // WCOLS, 2 * PH * 128 // WCOLS
PIECES = N_IN + N_OUT + N_Q
WRING = 3
EARLY = 8
EARLY_LOADS = EARLY + 2
UXBUF = 3
UBUF = 4
VBUF = 5
WORK = 6144
RING = 10

SLOPES = [2.0 ** (-8.0 * (h + 1) / HEADS) for h in range(HEADS)]


def rows(b):
    return CHUNK if b == SAMPLE else P


def u_slots(b):
    return SLOTS // 2 if b == SAMPLE else SLOTS


def u_before(b):
    return SLOTS * b


def v_before(b):
    return P * b


def v_token(b, i):
    groups = rows(b) // 32
    return 32 * (i % groups) + i // groups


PHASES = [
    ([0], []),
    ([1, 2], [(0, None), (None, 0)]),
    ([3, 4], [(1, None), (2, 1)]),
    ([5, 6], [(3, 2), (4, 3)]),
    ([7, 8], [(5, 4), (6, 5)]),
    ([], [(7, 6), (8, 7), (None, 8)]),
]


def place(b):
    return 2 if b == 0 else next(blocks.index(b) for blocks, _ in PHASES if b in blocks)


def sharing(b):
    return [c for c in range(b + 1) if place(c) == place(b)]


def gather_order():
    order = {}
    for _, segs in PHASES:
        for u, v in segs:
            for k in range(seg_len((u, v))):
                if u is not None and k < u_slots(u):
                    order["u", u_before(u) + k] = len(order)
                if v is not None and k < rows(v):
                    order["v", v_before(v) + k] = len(order)
    return order


def seg_len(seg):
    u, v = seg
    return max(u_slots(u) if u is not None else 0, rows(v) if v is not None else 0)


class Pace:

    NORM, PIECE, ATTN, PEER = 4, 3.5, 52, 60
    SPARE = 6

    def __init__(self, blocks, segs):
        g = len(blocks)
        begun = blocks == PHASES[1][0]
        self.slots = sum(seg_len(s) for s in segs)
        at, self.base = 0.0, {}
        for name, width in (("norm1", 0 if begun else g * self.NORM),
                            ("w_in", g * (N_IN - EARLY * begun) * self.PIECE), ("attn", g * self.ATTN),
                            ("w_out", g * N_OUT * self.PIECE), ("norm2", g * self.NORM),
                            ("w_q", g * N_Q * self.PIECE), ("peer", g * self.PEER)):
            self.base[name] = at
            at += width
        self.total = at
        self.floors, end = [], 0
        for seg in segs:
            end += seg_len(seg)
            if seg[0] is not None and seg[0] + UXBUF in blocks:
                self.floors.append((self.base["norm2"] + self.NORM * blocks.index(seg[0] + UXBUF), end))
        self.done = {"w_in": g * EARLY} if begun else {}
        self.width = {"norm1": self.NORM, "norm2": self.NORM, "attn": self.ATTN, "peer": self.PEER,
                      "w_in": self.PIECE, "w_out": self.PIECE, "w_q": self.PIECE}

    def slot(self, step, n, part=0.0):
        at = self.base[step] + self.width[step] * (n - self.done.get(step, 0) + part)
        n = int(at / self.total * (self.slots - self.SPARE)) if self.slots else 0
        return max([n] + [end for start, end in self.floors if at >= start])


def shape_constants():
    q = np.arange(P)
    k = np.arange(-WINDOW, P)
    qc, kc = q // CHUNK, k // CHUNK
    valid = (kc[None, :] <= qc[:, None]) & (kc[None, :] >= qc[:, None] - WINDOW // CHUNK)
    dist = np.where(valid, np.abs(q[:, None] - k[None, :]), MASKED_DIST).astype(np.float32)
    lg = np.log(1.0 - 2.0 ** (-5.0 - np.arange(RH))).astype(np.float32).astype(np.float64)
    scale = HD ** -0.5
    j, i = np.arange(P)[:, None], np.arange(P)[None, :]
    seen = (j // CHUNK) <= (i // CHUNK)
    decay = np.zeros((P, 2, RH // 2, P))
    gin = np.zeros((P, RH // 2, P))
    gout = np.zeros((P, 2, RH))
    gblk = np.zeros((P, 2, RH // 2))
    for h in range(RH):
        g = np.exp(lg[h])
        decay[:, h % 2, h // 2] = np.where(seen, g ** np.abs(i - j), 0.0) * scale
        half = slice(HD * (h % 2), HD * (h % 2) + HD)
        gin[half, h // 2] = g ** (np.arange(P) + 1.0)
        gout[:, 0, h] = g ** (P - 1.0 - np.arange(P)) * scale
        gout[:CHUNK, 1, h] = g ** (CHUNK - 1.0 - np.arange(CHUNK)) * scale
        gblk[half, 0, h // 2] = g ** P
        gblk[half, 1, h // 2] = g ** CHUNK
    iota = np.tile(np.arange(TOPK), (P, 1))
    parts = [dist, decay.reshape(P, -1), gin.reshape(P, -1), gout.reshape(P, -1), gblk.reshape(P, -1),
             iota, np.eye(P)]
    return np.concatenate([a.astype(np.float32) for a in parts], axis=1)


CONST_WIDTHS = [WINDOW + P, RH * P, RH // 2 * P, 2 * RH, RH, TOPK, P]


def hymba_peer_program(nc, x_prompt, x_sample, cache_attn_k, cache_attn_v, state_ret, attn_norm_g, w_in,
                       attn_sinks, ret_norm_g, w_out, ffn_norm_g, peer_w_q, peer_sub_keys, peer_u, peer_v,
                       final_norm_g, tables, y_prompt, y_sample, new_k_prompt, new_v_prompt, new_s_prompt,
                       new_k_sample, new_v_sample, new_s_sample):
    u_table, v_table = peer_u[0], peer_v[0]
    w_views = [w[0].rearrange("(k p) n -> p k n", p=P) for w in (w_in, w_out, peer_w_q)]

    def w_piece(n):
        if n < N_IN:
            view, n = w_views[0], n
        elif n < N_IN + N_OUT:
            view, n = w_views[1], n - N_IN
        else:
            view, n = w_views[2], n - N_IN - N_OUT
        return view[:, :, n * WCOLS:(n + 1) * WCOLS]

    def x_rows(b):
        return x_sample[0] if b == SAMPLE else x_prompt[0, b * P:(b + 1) * P, :]

    def y_rows(b):
        return y_sample[0] if b == SAMPLE else y_prompt[0, b * P:(b + 1) * P, :]

    x1_dram = nc.dram_tensor("x1_scratch", (NBLK, P, D), F32).ap()

    with ExitStack() as ctx:
        def sb(name, shape, dt=F32):
            return ctx.enter_context(nc.sbuf_tensor(name, shape, dt))

        def sem(name):
            return ctx.enter_context(nc.semaphore(name))

        const = sb("const", [P, sum(CONST_WIDTHS)])
        ends = np.cumsum(CONST_WIDTHS).tolist()
        cv = [const[:, e - w:e] for e, w in zip(ends, CONST_WIDTHS)]
        dist, ident, iota16 = cv[0], cv[6], cv[5]
        decay = cv[1].rearrange("p (e a i) -> p e a i", e=2, a=RH // 2)
        gin = cv[2].rearrange("p (a i) -> p a i", i=P)
        gout = cv[3].rearrange("p (s h) -> p s h", s=2)
        gblk = cv[4].rearrange("p (s a) -> p s a", s=2)

        g_attn = sb("g_attn", [P, D])
        g_ffn = sb("g_ffn", [P, D])
        g_fin = sb("g_fin", [P, D])
        g_ret = sb("g_ret", [P, RW])
        sinks = sb("sinks", [P, HEADS])
        wbuf = sb("wbuf", [P, WRING, KC, WCOLS])
        keysT = sb("keysT", [P, HC, NKEY])
        ring = sb("ring", [P, RING, D])
        x_in = sb("x_in", [P, 2, D])
        h_nat = sb("h_nat", [P, D])
        u_x = sb("u_x", [P, UXBUF, D])
        actT = sb("actT", [P, 2, KC, P])
        wide = sb("wide", [P, 2 * IN_W])
        early = ring[:, 2:5, :].rearrange("p r n -> p (r n)")
        x_of = {0: ring[:, 0, :]}
        act_of = {0: ring[:, 1, :].rearrange("p (k t) -> p k t", t=P)}
        proj_of, pq_of = {0: early[:, 0:IN_W]}, {0: early[:, 0:HC * P]}
        for blocks, _ in PHASES[1:]:
            for g, b in enumerate(blocks):
                x_of[b], act_of[b] = x_in[:, g, :], actT[:, g]
                proj_of[b] = wide[:, g * IN_W:(g + 1) * IN_W]
                pq_of[b] = wide[:, g * HC * P:(g + 1) * HC * P]
        work = sb("work", [P, WORK])
        off = [0]

        def part(n):
            off[0] += n
            assert off[0] <= WORK
            return work[:, off[0] - n:off[0]]

        KW = WINDOW + P
        scores = part(HEADS * KW).rearrange("p (h k) -> p h k", h=HEADS)
        qT = part(AW).rearrange("p (j q) -> p j q", q=P)
        qrT = part(RW).rearrange("p (a q) -> p a q", q=P)
        krT = part(RW).rearrange("p (a q) -> p a q", q=P)
        qrTs = part(RW).rearrange("p (a q) -> p a q", q=P)
        k_dec = part(RW)
        gate_e = part(RW)
        retP = part(RH * P).rearrange("p (e a i) -> p e a i", e=2, a=RH // 2)
        off[0] = HEADS * KW
        probsT = part(HEADS * KW).rearrange("p (h s q) -> p h s q", h=HEADS, s=2)
        off[0] += 2 * RW
        centred = part(RW)
        squares = part(RW)
        off[0] = 0
        pqT = part(HC * P).rearrange("p (c t) -> p c t", t=P)
        sims = part(HC * NKEY).rearrange("p (c n) -> p c n", n=NKEY)
        top_f = part(HC * TOPK).rearrange("p (c k) -> p c k", k=TOPK)
        pos_f = part(2 * SLOTS).rearrange("p (s n) -> p s n", s=2)
        half_f = part(2 * SLOTS).rearrange("p (s n) -> p s n", s=2)
        expert_f = part(SLOTS)
        top_v = part(HC * TOPK).rearrange("p (c k) -> p c k", k=TOPK)
        best_v = part(PH * TOPK).rearrange("p (h k) -> p h k", k=TOPK)
        top_i = part(HC * TOPK).bitcast(U32).rearrange("p (c k) -> p c k", k=TOPK)
        best_p = part(PH * TOPK).bitcast(U32).rearrange("p (h k) -> p h k", k=TOPK)
        pos_u = part(2 * SLOTS).bitcast(U32).rearrange("p (s n) -> p s n", s=2)
        off[0] = 0
        cand = part(PH * TOPK * TOPK).rearrange("p (h n) -> p h n", h=PH)
        onehot = part(PH * TOPK * TOPK).rearrange("p (h k i) -> p h k i", h=PH, k=TOPK)
        junk = work[:, 0:D]

        cache_kT = sb("cache_kT", [P, WINDOW])
        kT_win = sb("kT_win", [P, WINDOW + P])
        v_prev = sb("v_prev", [P, KVW])
        cache_k = sb("cache_k", [P, KVW])
        cache_v = sb("cache_v", [P, KVW])
        state = sb("state", [P, RH // 2, 2 * HD])
        state_s = sb("state_s", [P, RH // 2, HD])
        state_p = sb("state_p", [P, RH // 2, HD])
        stats = sb("stats", [P, 8, HEADS])
        row_max, neg_max, sink_e, den, rden, r_sum, r_var, r_std = (stats[:, i, :] for i in range(8))
        norm_s = sb("norm_s", [P, 8])
        g_stat = sb("g_stat", [P, 2, PH])

        u_idx = sb("u_idx", [P, UBUF, SLOTS], I32)
        v_idx = sb("v_idx", [P, VBUF, P], I32)
        u_gate = sb("u_gate", [P, UBUF, SLOTS])
        hidden = sb("hidden", [P, SLOTS])
        weight = sb("weight", [P, SLOTS])
        spread = sb("spread", [P, P * 32])
        x1_v = sb("x1_v", [P, D])
        fin_s = sb("fin_s", [P, 4])

        ps = ctx.enter_context(nc.psum_tensor("ps", [P, 8, 512], F32))
        B_WT, B_ACC = 5, 6

        consts_in = sem("consts_in")
        cache_in = sem("cache_in")
        keys_in = sem("keys_in")
        x_landed = [sem(f"x_landed{g}") for g in range(3)]
        w_landed = [sem(f"w_landed{i}") for i in range(WRING)]
        x1_stored = [sem(f"x1_stored{g}") for g in range(3)]
        sample_packed = sem("sample_packed")
        x1_in = sem("x1_in")
        landed = [sem(f"landed{i}") for i in range(RING)]
        y_stored = sem("y_stored")
        side_stored = sem("side_stored")
        vec_step = sem("vec_step")
        act_step = sem("act_step")
        cleared = sem("cleared")
        keys_tr = sem("keys_tr")
        keys_ready = sem("keys_ready")
        cache_tr = sem("cache_tr")
        kv_carried = sem("kv_carried")
        sq1_ready, ms1_ready, sd1_ready = sem("sq1_ready"), sem("ms1_ready"), sem("sd1_ready")
        h_ready, h_tr, hT_ready = sem("h_ready"), sem("h_tr"), sem("hT_ready")
        in_done, proj_ready = sem("in_done"), sem("proj_ready")
        qk_tr, qk_ready = sem("qk_tr"), sem("qk_ready")
        scores_done, scores_read = sem("scores_done"), sem("scores_read")
        max_ready, exp_ready, gate_exp = sem("max_ready"), sem("exp_ready"), sem("gate_exp")
        ret_done, retP_ready = sem("ret_done"), sem("retP_ready")
        or_done, kv_done, or_read = sem("or_done"), sem("kv_done"), sem("or_read")
        state_ready = sem("state_ready")
        var_ready, sd_ready = sem("var_ready"), sem("sd_ready")
        probs_tr, probsT_ready = sem("probs_tr"), sem("probsT_ready")
        ctx_done, mixed_ready = sem("ctx_done"), sem("mixed_ready")
        mix_tr, mixT_ready = sem("mix_tr"), sem("mixT_ready")
        out_done, x1_ready = sem("out_done"), sem("x1_ready")
        sq2_ready, ms2_ready, sd2_ready = sem("sq2_ready"), sem("ms2_ready"), sem("sd2_ready")
        h2_ready, h2_tr, h2T_ready = sem("h2_ready"), sem("h2_tr"), sem("h2T_ready")
        q_done, q_ready = sem("q_done"), sem("q_ready")
        pq_tr, pqT_ready = sem("pq_tr"), sem("pqT_ready")
        sims_done, sims_ready = sem("sims_done"), sem("sims_ready")
        gdiff_ready, gexp_ready = sem("gdiff_ready"), sem("gexp_ready")
        first_experts = sem("first_experts")
        expert_ready = sem("expert_ready")
        expert_tr, expertT_ready = sem("expert_tr"), sem("expertT_ready")
        dots_done = sem("dots_done")
        summed = sem("summed")
        gelu_ready, weight_ready, weight_tr, spread_ready = (
            sem("gelu_ready"), sem("weight_ready"), sem("weight_tr"), sem("spread_ready"))
        acc_read, fin_ms, fin_sd, y_ready = sem("acc_read"), sem("fin_ms"), sem("fin_sd"), sem("y_ready")

        block = ctx.enter_context(nc.Block())

        class Threader:

            def __init__(self, slot, end, before=None):
                self.slot, self.end, self.before = slot, end, before

            def phase(self, blocks, segs):
                self.pace = Pace(blocks, segs)
                self.todo = [(s, k) for s in segs for k in range(seg_len(s))]
                self.at = 0

            def upto(self, n):
                while self.at < min(n, len(self.todo)):
                    seg, k = self.todo[self.at]
                    if k == 0 and self.before:
                        self.before(seg)
                    self.slot(seg, k)
                    self.at += 1
                    if k == seg_len(seg) - 1:
                        self.end(seg)

            def step(self, name, n, part=0.0):
                self.upto(self.pace.slot(name, n, part))

            def rest(self):
                self.upto(len(self.todo))

        class Chain:

            def __init__(self, eng, own):
                self.eng, self.own, self.count, self.last = eng, own, {}, None

            def put(self, ins, signal=None):
                signal = signal or self.own
                ins.then_inc(signal, 1)
                self.count[signal.name] = self.count.get(signal.name, 0) + 1
                self.last = (signal, self.count[signal.name])

            def settle(self):
                self.eng.wait_ge(*self.last)

        following = PHASES[1][0]
        early_h = {3: 0, 6: 1}
        order = gather_order()
        gathers = {n: kind for kind, n in order.items()}

        def await_tile(eng, kind, n):
            at = order[kind, n]
            eng.wait_ge(landed[at % RING], 16 * (at // RING + 1))
            return ring[:, at % RING, :]

        def nothing(*_):
            pass

        @block.sync
        def _(sp):
            def load_piece(blocks, n):
                b0, G = blocks[0], len(blocks)
                m = n - WRING
                if m < 0 and b0:
                    sp.wait_ge(q_done, N_Q * b0)
                elif 0 <= m < N_IN:
                    sp.wait_ge(in_done, N_IN * b0 + (m + 1) * G)
                elif N_IN <= m < N_IN + N_OUT:
                    sp.wait_ge(out_done, N_OUT * b0 + (m - N_IN + 1) * G)
                elif m >= 0:
                    sp.wait_ge(q_done, N_Q * b0 + (m - N_IN - N_OUT + 1) * G)
                sp.dma_start(wbuf[:, n % WRING], w_piece(n)).then_inc(w_landed[n % WRING], 16)

            def stream(blocks, ns):
                b0, G = blocks[0], len(blocks)
                for n in ns:
                    m = n - WRING
                    if m < 0:
                        load_piece(blocks, n)
                        continue
                    name, first = (("w_in", 0) if m < N_IN else ("w_out", N_IN) if m < N_IN + N_OUT
                                   else ("w_q", N_IN + N_OUT))
                    if m == N_IN:
                        for g, b in enumerate(blocks):
                            if b >= SAMPLE - 1:
                                th.step("attn", g, 1.0)
                                store_window_and_state(b)
                    if m == N_IN + N_OUT:
                        for g, b in enumerate(blocks):
                            th.step("norm2", g)
                            T = rows(b)
                            sp.wait_ge(x1_ready, N_OUT * b0 + (N_OUT - 1) * G + g + 1)
                            sp.dma_start(x1_dram[b, 0:T, :], x_of[b][0:T, :]).then_inc(x1_stored[place(b)], 16)
                    th.step(name, (m - first) * G + G - 1, 0.5)
                    load_piece(blocks, n)

            def load_x(b):
                g, users = place(b), sharing(b)
                if len(users) > 1:
                    sp.wait_ge(h2_ready, users[-2] + 1)
                    sp.wait_ge(x1_stored[g], 16 * (len(users) - 1))
                sp.dma_start(x_of[b][0:rows(b), :], x_rows(b)).then_inc(x_landed[g], 16)

            def store_window_and_state(b):
                T = rows(b)
                sp.wait_ge(proj_ready, N_IN * NBLK)
                for c, old, dst_p, dst_s in ((C_KA, cache_k, new_k_prompt, new_k_sample),
                                             (C_VA, cache_v, new_v_prompt, new_v_sample)):
                    dst = (dst_s if b == SAMPLE else dst_p)[0, 0].rearrange("t h d -> t (h d)")
                    sp.dma_start(dst[WINDOW - T:WINDOW, :], proj_of[b][0:T, c:c + KVW]).then_inc(side_stored, 16)
                    if b == SAMPLE:
                        sp.wait_ge(cache_in, 64)
                        sp.dma_start(dst[0:WINDOW - T, :], old[T:WINDOW, :]).then_inc(side_stored, 16)
                sp.wait_ge(state_ready, b + 1)
                dst = (new_s_sample if b == SAMPLE else new_s_prompt)[0, 0].rearrange("(a e) d f -> e d a f", e=2)
                for e in range(2):
                    half = slice(HD * e, HD * e + HD)
                    src = state[half, :, half] if b == SAMPLE else state_p[half, :, :]
                    sp.dma_start(dst[e], src).then_inc(side_stored, 16)

            th = Threader(nothing, nothing)
            for blocks, segs in PHASES:
                th.phase(blocks, segs)
                th.upto(1)
                G = len(blocks)
                if not G:
                    th.rest()
                    continue
                b0 = blocks[0]
                if b0 == 0:
                    load_x(0)
                    sp.dma_start(const[:], tables).then_inc(consts_in, 16)
                    for t, src in ((g_attn, attn_norm_g[0]), (g_ffn, ffn_norm_g[0]), (g_ret, ret_norm_g[0]),
                                   (sinks, attn_sinks[0]), (g_fin, final_norm_g)):
                        sp.dma_start(t[:], src.partition_broadcast(P)).then_inc(consts_in, 16)
                    sp.dma_start(sims[:, :, :], peer_sub_keys[0].rearrange("h c n d -> n (h c) d")
                                 ).then_inc(keys_in, 16)
                    sp.dma_start(cache_k[:], cache_attn_k[0, 0].rearrange("t h d -> t (h d)")).then_inc(cache_in, 16)
                    sp.dma_start(cache_v[:], cache_attn_v[0, 0].rearrange("t h d -> t (h d)")).then_inc(cache_in, 16)
                    old = state_ret[0, 0].rearrange("(a e) d f -> e d a f", e=2)
                    for e in range(2):
                        half = slice(HD * e, HD * e + HD)
                        sp.dma_start(state_s[half, :, :], old[e]).then_inc(cache_in, 16)
                if b0 == 0:
                    stream(blocks, range(N_IN))
                    for b in following:
                        load_x(b)
                    stream(blocks, range(N_IN, PIECES))
                    stream(following, range(EARLY_LOADS))
                elif blocks == PHASES[1][0]:
                    stream(blocks, range(EARLY_LOADS, PIECES))
                else:
                    stream(blocks, range(WRING))
                    for b in blocks:
                        load_x(b)
                    stream(blocks, range(WRING, PIECES))
                if blocks[-1] == SAMPLE:
                    th.step("peer", G - 1, 0.98)
                    sp.wait_ge(expert_ready, 2 * NBLK)
                    low, high = slice(0, 64), slice(64, 128)
                    for buf, i, cols in ((u_idx, SAMPLE % UBUF, high), (u_gate, SAMPLE % UBUF, high),
                                         (u_x, SAMPLE % UXBUF, slice(0, D))):
                        width = cols.stop - cols.start
                        sp.dma_start(buf[high, i, 0:width], buf[low, i, cols]).then_inc(sample_packed, 16)
                th.rest()
            sp.wait_ge(y_stored, 16 * NBLK)
            sp.wait_ge(side_stored, 16 * 10)
            for b in (0, PROMPT_BLOCKS - 1, SAMPLE):
                sp.wait_ge(x1_stored[place(b)], 16 * len(sharing(b)))

        @block.gpsimd
        def _(pool):
            pool.memset(spread[:], 0.0).then_inc(cleared, 1)
            pool.memset(weight[:], 0.0).then_inc(cleared, 1)
            pool.memset(state[:, :, :], 0.0).then_inc(cleared, 1)

            def gather(at, table, idx):
                if at >= RING:
                    kind, n = gathers[at - RING]
                    pool.wait_ge(dots_done if kind == "u" else summed, n + 1)
                pool.indirect_dma_start(ring[:, at % RING, :], None, table,
                                        bass.IndirectOffsetOnAxis(ap=idx, axis=0)).then_inc(landed[at % RING], 16)

            def slot(seg, k):
                u, v = seg
                if u is not None and k < u_slots(u):
                    i, n = u % UBUF, u_before(u) + k
                    if u == 0 and k == 0:
                        pool.wait_ge(first_experts, 1)
                        pool.wait_ge(x1_stored[place(0)], 16)
                    if k == (SLOTS // 2 if u == 0 else 0):
                        pool.wait_ge(expert_ready, 2 * u + 1)
                        if u == SAMPLE:
                            pool.wait_ge(sample_packed, 48)
                    gather(order["u", n], u_table, u_idx[:, i, k:k + 1])
                if v is not None and k < rows(v):
                    i, n, t = v % VBUF, v_before(v) + k, v_token(v, k)
                    if k == 0:
                        pool.wait_ge(expertT_ready, v + 1)
                    gather(order["v", n], v_table, v_idx[:, i, t:t + 1])

            th = Threader(slot, nothing)
            for blocks, segs in PHASES:
                th.phase(blocks, segs)
                th.rest()

        @block.scalar
        def _(act):
            ch = Chain(act, act_step)
            copy = nc.scalar.copy

            def load_x1(seg):
                v = seg[1]
                if v is not None:
                    act.wait_ge(x1_stored[place(v)], 16 * len(sharing(v)))
                    if v:
                        act.wait_ge(y_stored, 16 * v)
                    act.dma_start(x1_v[0:rows(v), :], x1_dram[v, 0:rows(v), :]).then_inc(x1_in, 16)

            def end(seg):
                u, v = seg
                if u is not None:
                    n = u_slots(u)
                    act.wait_ge(dots_done, u_before(u) + n)
                    ch.put(nc.scalar.activation(hidden[:, 0:n], hidden[:, 0:n], ACT.Gelu), gelu_ready)
                if v is not None:
                    T = rows(v)
                    act.wait_ge(fin_ms, v + 1)
                    ch.put(nc.scalar.activation(fin_s[0:T, 2:3], fin_s[0:T, 1:2], ACT.Sqrt), fin_sd)
                    act.wait_ge(y_ready, v + 1)
                    act.dma_start(y_rows(v), x1_v[0:T, :]).then_inc(y_stored, 16)

            def square_sum(b, g, ms, sd, sq):
                T = rows(b)
                if ch.last:
                    ch.settle()
                ch.put(nc.scalar.activation(junk[0:T, :], x_of[b][0:T, :], ACT.Square,
                                            accum_out=norm_s[0:T, g:g + 1]), sq)
                act.wait_ge(ms, b + 1)
                ch.put(nc.scalar.activation(norm_s[0:T, 4 + g:5 + g], norm_s[0:T, 2 + g:3 + g], ACT.Sqrt), sd)

            def four(bank, T):
                return ps[:, bank, :].rearrange("p (c t) -> p c t", c=4)[:, :, 0:T]

            def squares_1(blocks):
                for g, b in enumerate(blocks):
                    th.step("norm1", g)
                    act.wait_ge(x_landed[place(b)], 16 * len(sharing(b)))
                    if b == 0:
                        act.wait_ge(cleared, 3)
                    square_sum(b, g, ms1_ready, sd1_ready, sq1_ready)

            def h_copied(g, b):
                T = rows(b)
                th.step("norm1", g, 0.5)
                for i in range(2):
                    act.wait_ge(h_tr, 2 * b + i + 1)
                    ch.put(copy(act_of[b][:, 4 * i:4 * i + 4, 0:T], four(i, T)), hT_ready)

            def projected(blocks, pieces):
                G = len(blocks)
                for p in pieces:
                    for g, b in enumerate(blocks):
                        m = p * G + g
                        th.step("w_in", m, 0.5)
                        act.wait_ge(in_done, N_IN * blocks[0] + m + 1)
                        T = rows(b)
                        dst, src = proj_of[b][0:T, p * WCOLS:(p + 1) * WCOLS], ps[0:T, 2 + m % 2, 0:WCOLS]
                        if p < KVH:
                            dst = proj_of[b][0:T, 0:AW].rearrange("p (j v d) -> p j v d", v=KVH, d=HD)[:, :, p, :]
                            src = src.rearrange("p (j d) -> p j d", d=HD)
                        ch.put(copy(dst, src), proj_ready)

            th = Threader(nothing, end, load_x1)
            for blocks, segs in PHASES:
                th.phase(blocks, segs)
                G = len(blocks)
                if not G:
                    th.rest()
                    continue
                b0 = blocks[0]
                begun = blocks == following
                if not begun:
                    squares_1(blocks)
                if b0 == 0:
                    for i in range(4):
                        act.wait_ge(keys_tr, i + 1)
                        ch.put(copy(keysT[:, 4 * i:4 * i + 4, :], four(i, P)), keys_ready)
                    act.wait_ge(cache_tr, 1)
                    ch.put(copy(cache_kT[:], ps[:, 4, 0:P]))
                if not begun:
                    for g, b in enumerate(blocks):
                        h_copied(g, b)
                projected(blocks, range(EARLY if begun else 0, N_IN))
                for g, b in enumerate(blocks):
                    T = rows(b)
                    lo, hi = (WINDOW if b == 0 else 0), WINDOW + T
                    th.step("attn", g, 0.05)
                    act.wait_ge(qk_tr, 4 * b + 1)
                    ch.put(nc.scalar.mul(qT[:, :, 0:T], four(0, T), HD ** -0.5), qk_ready)
                    act.wait_ge(qk_tr, 4 * b + 2)
                    if b:
                        ch.settle()
                    ch.put(copy(kT_win[:, WINDOW:WINDOW + T], ps[:, 1, 0:T]), qk_ready)
                    act.wait_ge(qk_tr, 4 * b + 3)
                    ch.put(copy(qrT[:, :, 0:T], four(2, T)), qk_ready)
                    act.wait_ge(qk_tr, 4 * b + 4)
                    ch.put(copy(krT[:, :, 0:T], four(3, T)), qk_ready)
                    ch.put(nc.scalar.activation(gate_e[0:T, :], proj_of[b][0:T, C_GT:C_GT + RW], ACT.Exp, scale=-1.0),
                           gate_exp)
                    th.step("attn", g, 0.25)
                    act.wait_ge(max_ready, b + 1)
                    for h in range(HEADS):
                        ch.put(nc.scalar.activation(scores[0:T, h, lo:hi], scores[0:T, h, lo:hi], ACT.Exp,
                                                    bias=neg_max[0:T, h:h + 1], accum_out=den[0:T, h:h + 1]))
                    ch.put(nc.scalar.activation(sink_e[0:T, :], sink_e[0:T, :], ACT.Exp), exp_ready)
                    th.step("attn", g, 0.55)
                    act.wait_ge(var_ready, b + 1)
                    ch.put(nc.scalar.activation(r_std[0:T, :], r_var[0:T, :], ACT.Sqrt), sd_ready)
                    th.step("attn", g, 0.65)
                    for i in range(4):
                        act.wait_ge(probs_tr, 4 * b + i + 1)
                        src = ps[:, i, :].rearrange("p (h s q) -> p h s q", h=2, s=2)
                        dst = probsT[:, 2 * i:2 * i + 2, :, :]
                        if b == 0:
                            ch.put(copy(dst[:, :, 1, :], src[:, :, 1, :]), probsT_ready)
                        elif b == SAMPLE:
                            ch.put(copy(dst[:, :, 0, 0:T], src[:, :, 0, 0:T]))
                            ch.put(copy(dst[0:T, :, 1, 0:T], src[0:T, :, 1, 0:T]), probsT_ready)
                        else:
                            ch.put(copy(dst, src), probsT_ready)
                    th.step("attn", g, 0.8)
                    if b < SAMPLE:
                        act.wait_ge(ctx_done, b + 1)
                        ch.settle()
                        cached = b + 1 == SAMPLE
                        if cached:
                            act.wait_ge(cache_in, 64)
                        ch.put(copy(kT_win[:, 0:WINDOW], cache_kT[:] if cached else kT_win[:, WINDOW:WINDOW + T]))
                        ch.put(copy(v_prev[:], cache_v[:] if cached else proj_of[b][:, C_VA:C_VA + KVW]), kv_carried)
                    th.step("attn", g, 0.9)
                    for i in range(2):
                        act.wait_ge(mix_tr, 2 * b + i + 1)
                        ch.put(copy(act_of[b][:, 4 * i:4 * i + 4, 0:T], four(i, T)), mixT_ready)
                for g, b in enumerate(blocks):
                    th.step("norm2", g)
                    act.wait_ge(x1_ready, N_OUT * b0 + (N_OUT - 1) * G + g + 1)
                    square_sum(b, g, ms2_ready, sd2_ready, sq2_ready)
                for g, b in enumerate(blocks):
                    T = rows(b)
                    th.step("norm2", g, 0.5)
                    for i in range(2):
                        act.wait_ge(h2_tr, 2 * b + i + 1)
                        ch.put(copy(act_of[b][:, 4 * i:4 * i + 4, 0:T], four(i, T)), h2T_ready)
                if b0 == 0:
                    squares_1(following)
                if blocks[-1] == SAMPLE:
                    act.wait_ge(side_stored, 16 * 10)
                for p in range(N_Q):
                    for g, b in enumerate(blocks):
                        m = p * G + g
                        th.step("w_q", m, 0.5)
                        act.wait_ge(q_done, N_Q * b0 + m + 1)
                        ch.put(copy(pq_of[b][0:rows(b), p * WCOLS:(p + 1) * WCOLS],
                                    ps[0:rows(b), 2 + m % 2, 0:WCOLS]), q_ready)
                        if b == 0 and m in early_h:
                            h_copied(early_h[m], following[early_h[m]])
                for g, b in enumerate(blocks):
                    T = rows(b)
                    th.step("peer", g)
                    if b:
                        act.wait_ge(expert_ready, 2 * b)
                    for i in range(4):
                        act.wait_ge(pq_tr, 4 * b + i + 1)
                        ch.put(copy(pqT[:, 4 * i:4 * i + 4, 0:T], four(i, T)), pqT_ready)
                    for i in range(4):
                        act.wait_ge(sims_done, 4 * b + i + 1)
                        ch.put(copy(sims[0:T, 4 * i:4 * i + 4, :], four(i, P)[0:T]), sims_ready)
                    if b == 0:
                        projected(following, range(EARLY - 2))
                    th.step("peer", g, 0.85)
                    act.wait_ge(gdiff_ready, b + 1)
                    ch.put(nc.scalar.activation(best_v[0:T, :, :], best_v[0:T, :, :], ACT.Exp), gexp_ready)
                    if b == 0:
                        projected(following, range(EARLY - 2, EARLY))
                th.rest()

        @block.vector
        def _(dve):
            ch = Chain(dve, vec_step)
            v_ = nc.vector

            def slot(seg, k):
                u = seg[0]
                if u is None or k >= u_slots(u):
                    return
                n = u_before(u) + k
                if k == 0:
                    dve.wait_ge(h2_ready, u + 1)
                    if u == SAMPLE:
                        dve.wait_ge(sample_packed, 48)
                row = await_tile(dve, "u", n)
                ch.put(v_.tensor_tensor_reduce(out=row, in0=row, in1=u_x[:, u % UXBUF, :], scale=1.0, scalar=0.0,
                                               op0=ALU.mult, op1=ALU.add, accum_out=hidden[:, k:k + 1]), dots_done)

            def end(seg):
                u, v = seg
                if v is not None:
                    T = rows(v)
                    dve.wait_ge(summed, v_before(v) + T)
                    dve.wait_ge(x1_in, 16 * (v + 1))
                    acc = ps[0:T, B_ACC:B_ACC + 2, :].rearrange("p a n -> p (a n)")
                    ch.put(v_.tensor_tensor(x1_v[0:T, :], x1_v[0:T, :], acc, ALU.add))
                    ch.settle()
                    ch.put(v_.tensor_tensor_reduce(out=acc, in0=x1_v[0:T, :], in1=x1_v[0:T, :], scale=1.0,
                                                   scalar=0.0, op0=ALU.mult, op1=ALU.add,
                                                   accum_out=fin_s[0:T, 0:1]), acc_read)
                if u is not None:
                    i = u % UBUF
                    dve.wait_ge(expert_ready, 2 * u + 2)
                    dve.wait_ge(gelu_ready, u + 1)
                    dve.wait_ge(cleared, 3)
                    if u:
                        dve.wait_ge(weight_tr, u)
                    if u != SAMPLE:
                        ch.put(v_.tensor_tensor(weight[:], hidden[:], u_gate[:, i, :], ALU.mult), weight_ready)
                    else:
                        ch.put(v_.memset(weight[:], 0.0))
                        ch.settle()
                        for half in (slice(0, 64), slice(64, 128)):
                            w = v_.tensor_tensor(weight[half, half], hidden[half, 0:64], u_gate[half, i, 0:64],
                                                 ALU.mult)
                        ch.put(w, weight_ready)
                    dve.wait_ge(weight_tr, u + 1)
                    if u:
                        dve.wait_ge(summed, v_before(u))
                    if u != SAMPLE:
                        dst = spread[:].rearrange("p (j c) -> p j c", j=4)[:, :, 0:1024:33]
                        ch.put(v_.tensor_copy(dst, ps[:, B_WT, 0:P].rearrange("p (j r) -> p j r", j=4)),
                               spread_ready)
                    else:
                        for half in (slice(0, 64), slice(64, 128)):
                            dst = spread[half, 0:2048].rearrange("p (j c) -> p j c", j=2)[:, :, 0:1024:33]
                            w = v_.tensor_copy(dst, ps[half, B_WT, half].rearrange("p (j r) -> p j r", j=2))
                        ch.put(w, spread_ready)
                if v is not None:
                    T = rows(v)
                    ch.settle()
                    ch.put(v_.tensor_scalar(fin_s[0:T, 1:2], fin_s[0:T, 0:1], 1.0 / D, EPS, ALU.mult, ALU.add), fin_ms)
                    dve.wait_ge(fin_sd, v + 1)
                    ch.put(v_.reciprocal(fin_s[0:T, 3:4], fin_s[0:T, 2:3]))
                    ch.settle()
                    ch.put(v_.scalar_tensor_tensor(out=x1_v[0:T, :], in0=x1_v[0:T, :], scalar=fin_s[0:T, 3:4],
                                                   in1=g_fin[0:T, :], op0=ALU.mult, op1=ALU.mult), y_ready)

            def norm(b, g, sq, ms, sd, gain, out, out_sem):
                T = rows(b)
                dve.wait_ge(sq, b + 1)
                ch.put(v_.tensor_scalar(norm_s[0:T, 2 + g:3 + g], norm_s[0:T, g:g + 1], 1.0 / D, EPS,
                                        ALU.mult, ALU.add), ms)
                dve.wait_ge(sd, b + 1)
                ch.put(v_.reciprocal(norm_s[0:T, 6 + g:7 + g], norm_s[0:T, 4 + g:5 + g]))
                ch.settle()

                def last():
                    ch.put(v_.scalar_tensor_tensor(out=out[0:T, :], in0=x_of[b][0:T, :],
                                                   scalar=norm_s[0:T, 6 + g:7 + g], in1=gain[0:T, :],
                                                   op0=ALU.mult, op1=ALU.mult), out_sem)
                return last

            def norm_1(blocks):
                for g, b in enumerate(blocks):
                    th.step("norm1", g)
                    last = norm(b, g, sq1_ready, ms1_ready, sd1_ready, g_attn, h_nat, h_ready)
                    if b:
                        dve.wait_ge(h_tr, 2 * b)
                        dve.wait_ge(mix_tr, 2 * blocks[0])
                    last()

            def per_head(ap, T, n):
                return ap[0:T, :].unsqueeze(2).broadcast_to([T, HEADS, n])

            def top16(values, best, where, T, count, tick):
                for half in range(2):
                    out = slice(8 * half, 8 * half + 8)
                    ch.settle()
                    for c in range(count):
                        ch.put(v_.max(best[0:T, c, out], values[0:T, c, :]))
                        tick()
                    ch.settle()
                    for c in range(count):
                        ch.put(v_.max_index(where[0:T, c, out], best[0:T, c, out], values[0:T, c, :]))
                        tick()
                    if half == 0:
                        ch.settle()
                        for c in range(count):
                            ch.put(v_.match_replace(values[0:T, c, :], best[0:T, c, out], values[0:T, c, :], -3.0e38))
                            tick()

            th = Threader(slot, end)
            dve.wait_ge(consts_in, 16 * 6)
            for blocks, segs in PHASES:
                th.phase(blocks, segs)
                G = len(blocks)
                if not G:
                    th.rest()
                    continue
                b0 = blocks[0]
                if blocks != following:
                    norm_1(blocks)
                for g, b in enumerate(blocks):
                    T = rows(b)
                    lo, hi = (WINDOW if b == 0 else 0), WINDOW + T
                    th.step("attn", g, 0.1)
                    dve.wait_ge(proj_ready, N_IN * b0 + (N_IN - 1) * G + g + 1)
                    ch.put(v_.tensor_tensor(k_dec[0:T, :].rearrange("p (h d) -> p h d", h=RH),
                                            proj_of[b][0:T, C_KR:C_KR + RW].rearrange("p (h d) -> p h d", h=RH),
                                            per_head(gout[:, 1 if b == SAMPLE else 0, :], T, HD), ALU.mult))
                    dve.wait_ge(qk_ready, 4 * b + 4)
                    ch.put(v_.tensor_tensor(qrTs[:, :, 0:T], qrT[:, :, 0:T], gin[:, :, 0:T], ALU.mult))
                    th.step("attn", g, 0.2)
                    for h in range(HEADS):
                        if h % 2 == 0:
                            dve.wait_ge(scores_done, 4 * b + h // 2 + 1)
                        c = (h % 2) * KW
                        ch.put(v_.scalar_tensor_tensor(out=scores[0:T, h, lo:hi], in0=dist[0:T, lo:hi],
                                                       scalar=-SLOPES[h], in1=ps[0:T, h // 2, c + lo:c + hi],
                                                       op0=ALU.mult, op1=ALU.add), scores_read if h % 2 else None)
                    ch.settle()
                    ch.put(v_.tensor_reduce(row_max[0:T, :], scores[0:T, :, lo:hi], AX_X, ALU.max))
                    ch.settle()
                    ch.put(v_.tensor_tensor(row_max[0:T, :], row_max[0:T, :], sinks[0:T, :], ALU.max))
                    ch.settle()
                    ch.put(v_.tensor_tensor(sink_e[0:T, :], sinks[0:T, :], row_max[0:T, :], ALU.subtract))
                    ch.put(v_.tensor_scalar(neg_max[0:T, :], row_max[0:T, :], -1.0, None, ALU.mult), max_ready)
                    th.step("attn", g, 0.35)
                    for e in range(2):
                        dve.wait_ge(ret_done, 2 * b + e + 1)
                        src = ps[0:T, e, :].rearrange("p (a i) -> p a i", i=P)[:, :, 0:T]
                        ch.put(v_.tensor_tensor(retP[0:T, e, :, 0:T], src, decay[0:T, e, :, 0:T], ALU.mult), retP_ready)
                    th.step("attn", g, 0.5)
                    dve.wait_ge(or_done, b + 1)
                    o_ps = ps[0:T, 2, :].rearrange("p (h d) -> p h d", h=RH)
                    cen = centred[0:T, :].rearrange("p (h d) -> p h d", h=RH)
                    sq = squares[0:T, :].rearrange("p (h d) -> p h d", h=RH)
                    ch.put(v_.tensor_reduce(r_sum[0:T, :], o_ps, AX_X, ALU.add))
                    ch.settle()
                    ch.put(v_.tensor_scalar(r_sum[0:T, :], r_sum[0:T, :], 1.0 / HD, None, ALU.mult))
                    ch.settle()
                    ch.put(v_.tensor_tensor(cen, o_ps, per_head(r_sum, T, HD), ALU.subtract), or_read)
                    ch.settle()
                    ch.put(v_.tensor_tensor(sq, cen, cen, ALU.mult))
                    ch.settle()
                    ch.put(v_.tensor_reduce(r_var[0:T, :], sq, AX_X, ALU.add))
                    ch.settle()
                    ch.put(v_.tensor_scalar(r_var[0:T, :], r_var[0:T, :], 1.0 / HD, EPS, ALU.mult, ALU.add), var_ready)
                    dve.wait_ge(kv_done, b + 1)
                    for e in range(2):
                        half = slice(HD * e, HD * e + HD)
                        ch.put(v_.tensor_tensor(
                            state[half, :, half], state[half, :, half],
                            gblk[half, 1 if b == SAMPLE else 0, :].unsqueeze(2).broadcast_to([HD, RH // 2, HD]),
                            ALU.mult))
                    ch.settle()
                    last_prompt = b + 1 == SAMPLE
                    for e in range(2):
                        half = slice(HD * e, HD * e + HD)
                        kv = ps[half, 3, :].rearrange("p (a f) -> p a f", a=RH // 2)[:, :, half]
                        dst = state_p[half, :, :] if last_prompt else state[half, :, half]
                        ch.put(v_.tensor_tensor(dst, state[half, :, half], kv, ALU.add),
                               state_ready if e and not last_prompt else None)
                    if last_prompt:
                        dve.wait_ge(cache_in, 64)
                        ch.settle()
                        for e in range(2):
                            half = slice(HD * e, HD * e + HD)
                            ch.put(v_.tensor_copy(state[half, :, half], state_s[half, :, :]),
                                   state_ready if e else None)
                    th.step("attn", g, 0.7)
                    dve.wait_ge(gate_exp, b + 1)
                    ch.put(v_.tensor_scalar(gate_e[0:T, :], gate_e[0:T, :], 1.0, None, ALU.add))
                    ch.settle()
                    ch.put(v_.reciprocal(gate_e[0:T, :], gate_e[0:T, :]))
                    ch.settle()
                    ch.put(v_.tensor_tensor(gate_e[0:T, :], gate_e[0:T, :], proj_of[b][0:T, C_GT:C_GT + RW], ALU.mult))
                    dve.wait_ge(sd_ready, b + 1)
                    ch.put(v_.reciprocal(r_std[0:T, :], r_std[0:T, :]))
                    ch.settle()
                    ch.put(v_.tensor_tensor(gate_e[0:T, :], gate_e[0:T, :], g_ret[0:T, :], ALU.mult))
                    ch.put(v_.tensor_tensor(cen, cen, per_head(r_std, T, HD), ALU.mult))
                    ch.settle()
                    dve.wait_ge(h_tr, 2 * (b0 + G))
                    if g:
                        dve.wait_ge(mix_tr, 2 * b)
                    ch.put(v_.tensor_tensor(h_nat[0:T, AW:AW + RW], centred[0:T, :], gate_e[0:T, :], ALU.mult))
                    dve.wait_ge(exp_ready, b + 1)
                    ch.put(v_.tensor_tensor(den[0:T, :], den[0:T, :], sink_e[0:T, :], ALU.add))
                    ch.settle()
                    ch.put(v_.reciprocal(rden[0:T, :], den[0:T, :]))
                    ch.settle()
                    th.step("attn", g, 0.85)
                    dve.wait_ge(ctx_done, b + 1)
                    ch.put(v_.tensor_tensor(h_nat[0:T, 0:AW].rearrange("p (h d) -> p h d", h=HEADS),
                                            ps[0:T, 4, :].rearrange("p (h d) -> p h d", h=HEADS),
                                            per_head(rden, T, HD), ALU.mult), mixed_ready)
                for p in range(N_OUT):
                    for g, b in enumerate(blocks):
                        m = p * G + g
                        th.step("w_out", m, 0.5)
                        T = rows(b)
                        dve.wait_ge(out_done, N_OUT * b0 + m + 1)
                        x = x_of[b][0:T, p * WCOLS:(p + 1) * WCOLS]
                        ch.put(v_.tensor_tensor(x, x, ps[0:T, 2 + m % 2, 0:WCOLS], ALU.add), x1_ready)
                for g, b in enumerate(blocks):
                    th.step("norm2", g)
                    last = norm(b, g, sq2_ready, ms2_ready, sd2_ready, g_ffn, u_x[:, b % UXBUF, :], h2_ready)
                    if b >= UXBUF:
                        dve.wait_ge(h2_tr, 2 * (b - UXBUF + 1))
                        dve.wait_ge(dots_done, u_before(b - UXBUF) + u_slots(b - UXBUF))
                    last()
                if b0 == 0:
                    norm_1(following)
                for g, b in enumerate(blocks):
                    T = rows(b)
                    th.step("peer", g, 0.1)
                    ticks = [0]

                    def tick():
                        ticks[0] += 1
                        if ticks[0] % 4 == 0:
                            th.step("peer", g, 0.1 + 0.6 * ticks[0] / (5 * (HC + PH)))

                    dve.wait_ge(sims_ready, 4 * b + 4)
                    if b >= UBUF:
                        dve.wait_ge(dots_done, u_before(b - UBUF) + u_slots(b - UBUF))
                        dve.wait_ge(weight_ready, b - UBUF + 1)
                    if b:
                        dve.wait_ge(expert_tr, b)
                    for h0, h1 in ((0, PH // 2), (PH // 2, PH)) if b == 0 else ((0, PH),):
                        H, c0, c1, e0, e1 = h1 - h0, 2 * h0, 2 * h1, TOPK * h0, TOPK * h1
                        top16(sims[:, c0:c1, :], top_v[:, c0:c1, :], top_i[:, c0:c1, :], T, 2 * H, tick)
                        ch.settle()
                        ch.put(v_.tensor_copy(top_f[0:T, c0:c1, :], top_i[0:T, c0:c1, :]))
                        pair = top_v[0:T, c0:c1, :].rearrange("p (h s) k -> p h s k", s=2)
                        shape = [T, H, TOPK, TOPK]
                        ch.put(v_.tensor_tensor(cand[0:T, h0:h1].rearrange("p h (i j) -> p h i j", i=TOPK),
                                                pair[:, :, 0, :].unsqueeze(3).broadcast_to(shape),
                                                pair[:, :, 1, :].unsqueeze(2).broadcast_to(shape), ALU.add))
                        top16(cand[:, h0:h1, :], best_v[:, h0:h1, :], best_p[:, h0:h1, :], T, H, tick)
                        ch.settle()
                        bh = best_v[0:T, h0:h1, :]
                        ch.put(v_.tensor_copy(g_stat[0:T, 0, h0:h1], best_v[0:T, h0:h1, 0]))
                        flat_p = best_p[0:T, h0:h1, :].rearrange("p h k -> p (h k)")
                        ch.put(v_.tensor_scalar(pos_u[0:T, 0, e0:e1], flat_p, 4, None, ALU.logical_shift_right))
                        ch.put(v_.tensor_scalar(pos_u[0:T, 1, e0:e1], flat_p, TOPK - 1, None, ALU.bitwise_and))
                        ch.settle()
                        ch.put(v_.tensor_tensor(bh, bh, g_stat[0:T, 0, h0:h1].unsqueeze(2).broadcast_to([T, H, TOPK]),
                                                ALU.subtract), gdiff_ready if h1 == PH else None)
                        ch.put(v_.tensor_copy(pos_f[0:T, :, e0:e1], pos_u[0:T, :, e0:e1]))
                        for s in range(2):
                            th.step("peer", g, 0.75 + 0.05 * s)
                            ch.settle()
                            hot4 = onehot[0:T, h0:h1]
                            hot = hot4.rearrange("p h k i -> p (h k) i")
                            wide_shape = [T, e1 - e0, TOPK]
                            ch.put(v_.tensor_tensor(hot, iota16[0:T].unsqueeze(1).broadcast_to(wide_shape),
                                                    pos_f[0:T, s, e0:e1].unsqueeze(2).broadcast_to(wide_shape),
                                                    ALU.is_equal))
                            ch.settle()
                            num = top_f[0:T, c0:c1, :].rearrange("p (h s) k -> p h s k", s=2)[:, :, s, :]
                            ch.put(v_.tensor_tensor(hot4, hot4, num.unsqueeze(2).broadcast_to(shape), ALU.mult))
                            ch.settle()
                            ch.put(v_.tensor_reduce(half_f[0:T, s, e0:e1], hot, AX_X, ALU.add))
                        ch.settle()
                        ch.put(v_.scalar_tensor_tensor(out=expert_f[0:T, e0:e1], in0=half_f[0:T, 0, e0:e1],
                                                       scalar=float(NKEY), in1=half_f[0:T, 1, e0:e1], op0=ALU.mult,
                                                       op1=ALU.add))
                        ch.settle()
                        ch.put(v_.tensor_copy(u_idx[0:T, b % UBUF, e0:e1], expert_f[0:T, e0:e1]),
                               expert_ready if h1 == PH else first_experts)
                    bv = best_v[0:T, :, :]
                    th.step("peer", g, 0.9)
                    dve.wait_ge(gexp_ready, b + 1)
                    ch.put(v_.tensor_reduce(g_stat[0:T, 0, :], bv, AX_X, ALU.add))
                    ch.settle()
                    ch.put(v_.reciprocal(g_stat[0:T, 1, :], g_stat[0:T, 0, :]))
                    ch.settle()
                    ch.put(v_.tensor_tensor(u_gate[0:T, b % UBUF, :].rearrange("p (h k) -> p h k", h=PH), bv,
                                            g_stat[0:T, 1, :].unsqueeze(2).broadcast_to([T, PH, TOPK]), ALU.mult),
                           expert_ready)
                    th.step("peer", g, 0.98)
                    dve.wait_ge(expert_tr, b + 1)
                    if b >= VBUF:
                        dve.wait_ge(summed, v_before(b - VBUF) + rows(b - VBUF))
                    ch.put(v_.tensor_copy(v_idx[:, b % VBUF, 0:T], ps[:, 4, 0:T]), expertT_ready)
                th.rest()

        @block.tensor
        def _(pe):
            def slot(seg, k):
                v = seg[1]
                if v is None or k >= rows(v):
                    return
                n, t = v_before(v) + k, v_token(v, k)
                if k == 0:
                    pe.wait_ge(spread_ready, v + 1)
                    if v:
                        pe.wait_ge(acc_read, v)
                tile = await_tile(pe, "v", n)
                j = 32 * (t // 32)
                for c in range(2):
                    mm = pe.matmul(ps[j:j + 32, B_ACC + c, :], spread[:, 32 * t:32 * t + 32],
                                   tile[:, 512 * c:512 * c + 512], start=(t % 32 == 0),
                                   stop=(t % 32 == 31), skip_group_check=True)
                mm.then_inc(summed, 1)

            def end(seg):
                u = seg[0]
                if u is not None:
                    pe.wait_ge(weight_ready, u + 1)
                    if u:
                        pe.wait_ge(spread_ready, u)
                    pe.transpose(ps[:, B_WT, 0:P], weight[:], ident).then_inc(weight_tr, 1)

            def transposed(bank, T, src, count, signal, width=P):
                for c in range(count):
                    mm = pe.transpose(ps[0:width, bank, c * P:c * P + T], src(c), ident[0:T, 0:T])
                mm.then_inc(signal, 1)

            def h_transposed(g, b, free, count):
                T = rows(b)
                th.step("norm1", g, 0.5)
                pe.wait_ge(h_ready, b + 1)
                if b:
                    pe.wait_ge(hT_ready, 2 * b)
                    pe.wait_ge(free, count)
                for i in range(2):
                    transposed(i, T, lambda c: h_nat[0:T, (4 * i + c) * P:(4 * i + c + 1) * P], 4, h_tr)

            def project(blocks, grp, pieces):
                G = len(blocks)
                for p in pieces:
                    for g, b in enumerate(blocks):
                        m = p * G + g
                        th.step("w_in", m)
                        pe.wait_ge(hT_ready, 2 * b + 2)
                        if m >= 2:
                            pe.wait_ge(proj_ready, N_IN * blocks[0] + m - 1)
                        product(grp, "w_in", 0, p, m, b, in_done)

            def product(grp, name, first, p, m, b, signal):
                n, T = first + p, rows(b)
                pe.wait_ge(w_landed[n % WRING], 16 * (grp * len(range(n % WRING, PIECES, WRING)) + n // WRING + 1))
                for k in range(KC):
                    if k == KC // 2:
                        th.step(name, m, 0.5)
                    mm = pe.matmul(ps[0:T, 2 + m % 2, 0:WCOLS], act_of[b][:, k, 0:T], wbuf[:, n % WRING, k, :],
                                   start=(k == 0), stop=(k == KC - 1))
                mm.then_inc(signal, 1)

            th = Threader(slot, end)
            pe.wait_ge(consts_in, 16 * 6)
            grp = 0
            for blocks, segs in PHASES:
                th.phase(blocks, segs)
                G = len(blocks)
                if not G:
                    th.rest()
                    continue
                b0 = blocks[0]
                if b0 == 0:
                    pe.wait_ge(keys_in, 16)
                    for i in range(4):
                        transposed(i, P, lambda c: sims[:, 4 * i + c, :], 4, keys_tr)
                    pe.wait_ge(cache_in, 64)
                    transposed(4, P, lambda c: cache_k[:], 1, cache_tr)
                    pe.wait_ge(keys_ready, 4)
                begun = blocks == following
                if not begun:
                    for g, b in enumerate(blocks):
                        h_transposed(g, b, sims_ready, 4 * b0)
                project(blocks, grp, range(EARLY if begun else 0, N_IN))
                for g, b in enumerate(blocks):
                    T = rows(b)
                    lo, hi = (WINDOW if b == 0 else 0), WINDOW + T
                    pr = proj_of[b]
                    th.step("attn", g)
                    pe.wait_ge(proj_ready, N_IN * (b0 + G))
                    if g:
                        pe.wait_ge(mixT_ready, 2 * b)
                    transposed(0, T, lambda c: pr[0:T, c * P:(c + 1) * P], 4, qk_tr)
                    transposed(1, T, lambda c: pr[0:T, C_KA:C_KA + KVW], 1, qk_tr)
                    transposed(2, T, lambda c: pr[0:T, C_QR + c * P:C_QR + (c + 1) * P], 4, qk_tr)
                    transposed(3, T, lambda c: pr[0:T, C_KR + c * P:C_KR + (c + 1) * P], 4, qk_tr)
                    th.step("attn", g, 0.15)
                    pe.wait_ge(qk_ready, 4 * b + 4)
                    if b:
                        pe.wait_ge(kv_carried, b)
                    for h in range(HEADS):
                        half = slice(HD * (h // 4), HD * (h // 4) + HD)
                        c = (h % 2) * KW
                        mm = pe.matmul(ps[0:T, h // 2, c + lo:c + hi], qT[half, h % 4, 0:T], kT_win[half, lo:hi],
                                       start=True, stop=True)
                        if h % 2:
                            mm.then_inc(scores_done, 1)
                    th.step("attn", g, 0.3)
                    for e in range(2):
                        pe.wait_ge(scores_read, 4 * b + e + 1)
                        half = slice(HD * e, HD * e + HD)
                        for a in range(RH // 2):
                            mm = pe.matmul(ps[0:T, e, a * P:a * P + T], krT[half, a, 0:T], qrT[half, a, 0:T],
                                           start=True, stop=True)
                        mm.then_inc(ret_done, 1)
                    th.step("attn", g, 0.45)
                    pe.wait_ge(scores_read, 4 * b + 4)
                    pe.wait_ge(retP_ready, 2 * b + 2)
                    if b:
                        pe.wait_ge(state_ready, b)
                    else:
                        pe.wait_ge(cleared, 3)
                    for a in range(RH // 2):
                        pe.matmul(ps[0:T, 2, a * P:(a + 1) * P], qrTs[:, a, 0:T], state[:, a, :],
                                  start=True, stop=False, skip_group_check=True)
                        for e in range(2):
                            h = 2 * a + e
                            mm = pe.matmul(ps[0:T, 2, h * HD:(h + 1) * HD], retP[0:T, e, a, 0:T],
                                           pr[0:T, C_VR + h * HD:C_VR + (h + 1) * HD], start=False, stop=(e == 1),
                                           skip_group_check=True)
                    mm.then_inc(or_done, 1)
                    for a in range(RH // 2):
                        mm = pe.matmul(ps[:, 3, a * P:(a + 1) * P], k_dec[0:T, a * P:(a + 1) * P],
                                       pr[0:T, C_VR + a * P:C_VR + (a + 1) * P], start=True, stop=True)
                    mm.then_inc(kv_done, 1)
                    th.step("attn", g, 0.6)
                    pe.wait_ge(exp_ready, b + 1)
                    for i in range(4):
                        if i == 2:
                            pe.wait_ge(or_read, b + 1)
                        if i == 3:
                            pe.wait_ge(state_ready, b + 1)
                        for h in (2 * i, 2 * i + 1):
                            for s in range(2):
                                keys = T if s else WINDOW
                                if b == 0 and s == 0:
                                    continue
                                c = (2 * (h % 2) + s) * P
                                mm = pe.transpose(ps[0:keys, i, c:c + T], scores[0:T, h, s * WINDOW:s * WINDOW + keys],
                                                  ident[0:T, 0:T])
                        mm.then_inc(probs_tr, 1)
                    th.step("attn", g, 0.75)
                    pe.wait_ge(probsT_ready, 4 * b + 4)
                    if b:
                        pe.wait_ge(mixed_ready, b)
                        pe.wait_ge(expertT_ready, b0)
                    for h in range(HEADS):
                        v0 = HD * (h // 4)
                        out = ps[0:T, 4, h * HD:(h + 1) * HD]
                        if b:
                            pe.matmul(out, probsT[:, h, 0, 0:T], v_prev[:, v0:v0 + HD], start=True, stop=False)
                        mm = pe.matmul(out, probsT[0:T, h, 1, 0:T], pr[0:T, C_VA + v0:C_VA + v0 + HD],
                                       start=(b == 0), stop=True)
                    mm.then_inc(ctx_done, 1)
                    th.step("attn", g, 0.9)
                    pe.wait_ge(mixed_ready, b + 1)
                    for i in range(2):
                        transposed(i, T, lambda c: h_nat[0:T, (4 * i + c) * P:(4 * i + c + 1) * P], 4, mix_tr)
                for p in range(N_OUT):
                    for g, b in enumerate(blocks):
                        m = p * G + g
                        th.step("w_out", m)
                        pe.wait_ge(mixT_ready, 2 * b + 2)
                        if m >= 2:
                            pe.wait_ge(x1_ready, N_OUT * b0 + m - 1)
                        product(grp, "w_out", N_IN, p, m, b, out_done)
                for g, b in enumerate(blocks):
                    T = rows(b)
                    th.step("norm2", g, 0.5)
                    pe.wait_ge(h2_ready, b + 1)
                    pe.wait_ge(mixT_ready, 2 * (b0 + G))
                    if g:
                        pe.wait_ge(h2T_ready, 2 * b)
                    for i in range(2):
                        transposed(i, T, lambda c: u_x[0:T, b % UXBUF, (4 * i + c) * P:(4 * i + c + 1) * P], 4, h2_tr)
                for p in range(N_Q):
                    for g, b in enumerate(blocks):
                        m = p * G + g
                        th.step("w_q", m)
                        pe.wait_ge(h2T_ready, 2 * b + 2)
                        if m < 2:
                            pe.wait_ge(x1_ready, N_OUT * (b0 + G))
                        else:
                            pe.wait_ge(q_ready, N_Q * b0 + m - 1)
                        product(grp, "w_q", N_IN + N_OUT, p, m, b, q_done)
                        if b == 0 and m in early_h:
                            h_transposed(early_h[m], following[early_h[m]], h2T_ready, 2)
                for g, b in enumerate(blocks):
                    T = rows(b)
                    th.step("peer", g)
                    pe.wait_ge(q_ready, N_Q * (b0 + G))
                    pe.wait_ge(h2T_ready, 2 * (b0 + G))
                    if b == 0:
                        pe.wait_ge(hT_ready, 2 * (following[-1] + 1))
                    if g:
                        pe.wait_ge(sims_ready, 4 * b)
                    for i in range(4):
                        transposed(i, T, lambda c: pq_of[b][0:T, (4 * i + c) * P:(4 * i + c + 1) * P], 4, pq_tr)
                    pe.wait_ge(pqT_ready, 4 * b + 4)
                    for c in range(HC):
                        mm = pe.matmul(ps[0:T, c // 4, (c % 4) * P:(c % 4 + 1) * P], pqT[:, c, 0:T], keysT[:, c, :],
                                       start=True, stop=True)
                        if c % 4 == 3:
                            mm.then_inc(sims_done, 1)
                    if b == 0:
                        pe.wait_ge(sims_ready, 4)
                        project(following, grp + 1, range(EARLY))
                    th.step("peer", g, 0.95)
                    pe.wait_ge(expert_ready, 2 * b + 1)
                    transposed(4, T, lambda c: expert_f[0:T, :], 1, expert_tr)
                th.rest()
                grp += 1


_INS = ["x_prompt", "x_sample", "cache_attn_k", "cache_attn_v", "state_ret", "attn_norm_g", "w_in", "attn_sinks",
        "ret_norm_g", "w_out", "ffn_norm_g", "peer_w_q", "peer_sub_keys", "peer_u", "peer_v", "final_norm_g"]
_OUTS = [(1, 1024, D), (1, CHUNK, D), (1, 1, WINDOW, KVH, HD), (1, 1, WINDOW, KVH, HD), (1, 1, RH, HD, HD),
         (1, 1, WINDOW, KVH, HD), (1, 1, WINDOW, KVH, HD), (1, 1, RH, HD, HD)]


def kernel(**inputs):
    import concourse.bacc as _bacc
    from concourse.bass_utils import run_bass_kernel_spmd as _run

    nc = _bacc.Bacc("TRN2", target_bir_lowering=False, num_devices=1)
    arrays, args = {}, []
    feeds = [(name, np.ascontiguousarray(inputs[name])) for name in _INS] + [("tables", shape_constants())]
    for name, a in feeds:
        arrays[f"in_{name}_dram"] = a
        args.append(nc.dram_tensor(f"in_{name}_dram", a.shape, mybir.dt.from_np(a.dtype), kind="ExternalInput").ap())
    for i, shape in enumerate(_OUTS):
        args.append(nc.dram_tensor(f"out_{i}_dram", shape, F32, kind="ExternalOutput").ap())
    hymba_peer_program(nc, *args)
    r = _run(nc, [arrays], core_ids=[0])
    return tuple(r.results[0][f"out_{i}_dram"] for i in range(len(_OUTS)))
```
